# Optimizing a Trainium2 kernel written in Bass

```python
import functools
import jax, jax.numpy as jnp
from jax import lax
import numpy as np

D_MODEL = 2048
BATCH = 1
SEQ = 512
DEPTH = 1
DEC_BATCH = 1
DEC_SEQ = 32
PAST_LEN = 128

CHUNK = 64
LEFT_CHUNKS = 8
WINDOW = LEFT_CHUNKS * CHUNK
BAND = (LEFT_CHUNKS + 1) * CHUNK
HEAD_DIM = 128
D_A = D_MODEL // 2
N_HEADS_A = D_A // HEAD_DIM
D_M = D_MODEL // 4
N_HEADS_M = D_M // HEAD_DIM
N_MEM = 256
D_RNN = D_MODEL // 4
N_RNN_BLOCKS = 8
RNN_BLOCK = D_RNN // N_RNN_BLOCKS
CONV_B = 4
LRU_C = 8.0
D_FF = 3 * D_MODEL
CONV_F = 3
REL_CLIP = 256
EPS = 1e-6
D_MIX = D_A + D_M + D_RNN
D_IN = 3 * D_A + D_M + 2 * D_RNN
SPLITS = (D_A, 2 * D_A, 3 * D_A, 3 * D_A + D_M, 3 * D_A + D_M + D_RNN)
NEG = -1e30

kernel_name = 'hybrid_stream_chunk_encoder'

def rmsnorm(x, g):
    xf = x.astype(jnp.float32)
    y = xf * lax.rsqrt(jnp.mean(xf * xf, axis=-1, keepdims=True) + EPS)
    return (y * g.astype(jnp.float32)).astype(x.dtype)

def causal_dwconv(x, past, w, b):
    width = w.shape[0]
    t = x.shape[1]
    xp = jnp.concatenate([past, x], axis=1)
    y = b
    for k in range(width):
        y = y + w[k] * xp[:, k:k + t]
    return y, xp[:, -(width - 1):]

def softmax_attend(q, k, v, bias):
    s = jnp.einsum('...qhd,...khd->...hqk', q, k).astype(jnp.float32) * (HEAD_DIM ** -0.5) + bias
    p = jax.nn.softmax(s, axis=-1)
    return jnp.einsum('...hqk,...khd->...qhd', p.astype(v.dtype), v)

def rel_bias(table, dist):
    idx = jnp.clip(dist, -REL_CLIP, REL_CLIP) + REL_CLIP
    return jnp.take(table, idx, axis=1).astype(jnp.float32)

def band_attention_prompt(q, k, v, rel_table):
    b, s, h, dh = q.shape
    nc = s // CHUNK
    pad = ((0, 0), (WINDOW, 0), (0, 0), (0, 0))
    kp = jnp.pad(k, pad)
    vp = jnp.pad(v, pad)
    idx = jnp.arange(nc)[:, None] * CHUNK + jnp.arange(BAND)[None, :]
    kb = kp[:, idx]
    vb = vp[:, idx]
    qb = q.reshape(b, nc, CHUNK, h, dh)
    dist = jnp.arange(CHUNK)[:, None] + WINDOW - jnp.arange(BAND)[None, :]
    valid = jnp.where(idx >= WINDOW, 0.0, NEG).astype(jnp.float32)
    bias = rel_bias(rel_table, dist)[None] + valid[:, None, None, :]
    out = softmax_attend(qb, kb, vb, bias[None])
    return out.reshape(b, s, h, dh)

def band_attention_sample(q, k, v, k_past, v_past, rel_table):
    p_len = k_past.shape[1]
    t = q.shape[1]
    kk = jnp.concatenate([k_past, k], axis=1)
    vv = jnp.concatenate([v_past, v], axis=1)
    dist = (p_len + jnp.arange(t))[:, None] - jnp.arange(p_len + t)[None, :]
    return softmax_attend(q, kk, vv, rel_bias(rel_table, dist)[None])

def memory_kv(mem, g_mem, w_mem_kv, g_k_m):
    b, n, _ = mem.shape
    k, v = jnp.split(rmsnorm(mem, g_mem) @ w_mem_kv, 2, axis=-1)
    k = rmsnorm(k.reshape(b, n, N_HEADS_M, HEAD_DIM), g_k_m)
    return k, v.reshape(b, n, N_HEADS_M, HEAD_DIM)

def _lin_combine(left, right):
    a1, b1 = left
    a2, b2 = right
    return a1 * a2, a2 * b1 + b2

def rg_lru(x, h0, w_a, b_a, w_i, b_i, lam):
    b, t, _ = x.shape
    xb = x.reshape(b, t, N_RNN_BLOCKS, RNN_BLOCK)

    def gate(w, bias):
        z = jnp.einsum('btni,nij->btnj', xb, w).reshape(b, t, D_RNN) + bias
        return jax.nn.sigmoid(z.astype(jnp.float32))

    r = gate(w_a, b_a)
    i = gate(w_i, b_i)
    log_a = -LRU_C * r * jax.nn.softplus(-lam.astype(jnp.float32))
    a = jnp.exp(log_a)
    u = jnp.sqrt(-jnp.expm1(2.0 * log_a)) * (i * x.astype(jnp.float32))
    a_cum, b_cum = lax.associative_scan(_lin_combine, (a, u), axis=1)
    h = a_cum * h0.astype(jnp.float32)[:, None] + b_cum
    return h.astype(x.dtype), h[:, -1].astype(x.dtype)

def trunk_layer(x, attn_a, mem_k, mem_v, b_conv_past, b_h0, f_conv_past,
                g_attn, w_in, g_q_a, g_k_a, g_q_m, conv_b_w, conv_b_b,
                w_rg_a, b_rg_a, w_rg_i, b_rg_i, lru_lambda, w_out,
                g_ffn, w_up, conv_f_w, conv_f_b, w_down):
    b, t, _ = x.shape
    z = rmsnorm(x, g_attn) @ w_in
    q_a, k_a, v_a, q_m, x_b, g_b = jnp.split(z, SPLITS, axis=-1)
    q_a = rmsnorm(q_a.reshape(b, t, N_HEADS_A, HEAD_DIM), g_q_a)
    k_a = rmsnorm(k_a.reshape(b, t, N_HEADS_A, HEAD_DIM), g_k_a)
    v_a = v_a.reshape(b, t, N_HEADS_A, HEAD_DIM)
    o_a = attn_a(q_a, k_a, v_a).reshape(b, t, D_A)
    q_m = rmsnorm(q_m.reshape(b, t, N_HEADS_M, HEAD_DIM), g_q_m)
    o_m = softmax_attend(q_m, mem_k, mem_v, 0.0).reshape(b, t, D_M)
    xc, b_conv_new = causal_dwconv(x_b, b_conv_past, conv_b_w, conv_b_b)
    h, b_h_new = rg_lru(xc, b_h0, w_rg_a, b_rg_a, w_rg_i, b_rg_i, lru_lambda)
    o_b = h * jax.nn.gelu(g_b)
    x = x + jnp.concatenate([o_a, o_m, o_b], axis=-1) @ w_out
    up = rmsnorm(x, g_ffn) @ w_up
    up, f_conv_new = causal_dwconv(up, f_conv_past, conv_f_w, conv_f_b)
    val, gt = jnp.split(up, 2, axis=-1)
    x = x + (jax.nn.gelu(gt) * val) @ w_down
    return x, k_a, v_a, b_conv_new, b_h_new, f_conv_new

def setup_inputs(seed: int = 0) -> dict:
    key = jax.random.key(seed)
    keys = jax.random.split(key, 40)
    counter = [0]
    f32 = jnp.float32

    def nk():
        k = keys[counter[0]]
        counter[0] += 1
        return k

    def nrm(shape, scale=1.0):
        return jax.random.normal(nk(), shape, f32) * scale

    def gain(shape):
        return 1.0 + 0.1 * nrm(shape)

    L = DEPTH
    a_rows = min(WINDOW, PAST_LEN)
    inputs = {
        'x_prompt': nrm((BATCH, SEQ, D_MODEL)),
        'x_sample': nrm((DEC_BATCH, DEC_SEQ, D_MODEL)),
        'cache_a_k': nrm((L, DEC_BATCH, a_rows, N_HEADS_A, HEAD_DIM)),
        'cache_a_v': nrm((L, DEC_BATCH, a_rows, N_HEADS_A, HEAD_DIM)),
        'cache_mem_k': nrm((L, DEC_BATCH, N_MEM, N_HEADS_M, HEAD_DIM)),
        'cache_mem_v': nrm((L, DEC_BATCH, N_MEM, N_HEADS_M, HEAD_DIM)),
        'cache_b_conv': nrm((L, DEC_BATCH, CONV_B - 1, D_RNN)),
        'state_b_h': nrm((L, DEC_BATCH, D_RNN), 0.5),
        'cache_f_conv': nrm((L, DEC_BATCH, CONV_F - 1, 2 * D_FF)),
        'mem_prompt': nrm((BATCH, N_MEM, D_MODEL)),
        'g_attn': gain((L, D_MODEL)),
        'w_in': nrm((L, D_MODEL, D_IN), D_MODEL ** -0.5),
        'g_q_a': gain((L, HEAD_DIM)),
        'g_k_a': gain((L, HEAD_DIM)),
        'rel_table': nrm((L, N_HEADS_A, 2 * REL_CLIP + 1), 0.3),
        'g_q_m': gain((L, HEAD_DIM)),
        'g_k_m': gain((L, HEAD_DIM)),
        'g_mem': gain((L, D_MODEL)),
        'w_mem_kv': nrm((L, D_MODEL, 2 * D_M), D_MODEL ** -0.5),
        'conv_b_w': nrm((L, CONV_B, D_RNN), CONV_B ** -0.5),
        'conv_b_b': nrm((L, D_RNN), 0.02),
        'w_rg_a': nrm((L, N_RNN_BLOCKS, RNN_BLOCK, RNN_BLOCK), RNN_BLOCK ** -0.5),
        'b_rg_a': nrm((L, D_RNN), 0.02),
        'w_rg_i': nrm((L, N_RNN_BLOCKS, RNN_BLOCK, RNN_BLOCK), RNN_BLOCK ** -0.5),
        'b_rg_i': nrm((L, D_RNN), 0.02),
    }
    a0 = jax.random.uniform(nk(), (L, D_RNN), f32, 0.9, 0.999)
    s = a0 ** (1.0 / LRU_C)
    inputs['lru_lambda'] = jnp.log(s) - jnp.log1p(-s)
    inputs['w_out'] = nrm((L, D_MIX, D_MODEL), D_MIX ** -0.5)
    inputs['g_ffn'] = gain((L, D_MODEL))
    inputs['w_up'] = nrm((L, D_MODEL, 2 * D_FF), D_MODEL ** -0.5)
    inputs['conv_f_w'] = nrm((L, CONV_F, 2 * D_FF), CONV_F ** -0.5)
    inputs['conv_f_b'] = nrm((L, 2 * D_FF), 0.02)
    inputs['w_down'] = nrm((L, D_FF, D_MODEL), D_FF ** -0.5)
    return inputs

def reference(x_prompt, x_sample, cache_a_k, cache_a_v, cache_mem_k, cache_mem_v,
              cache_b_conv, state_b_h, cache_f_conv, mem_prompt,
              g_attn, w_in, g_q_a, g_k_a, rel_table, g_q_m, g_k_m, g_mem, w_mem_kv,
              conv_b_w, conv_b_b, w_rg_a, b_rg_a, w_rg_i, b_rg_i, lru_lambda,
              w_out, g_ffn, w_up, conv_f_w, conv_f_b, w_down):
    xp, xs = x_prompt, x_sample
    bp, sp, _ = xp.shape
    keep = min(WINDOW, sp)
    ak_p, av_p, mk_p, mv_p, bc_p, bh_p, fc_p = [], [], [], [], [], [], []
    ak_s, av_s, bc_s, bh_s, fc_s = [], [], [], [], []
    for l in range(DEPTH):
        shared = (g_attn[l], w_in[l], g_q_a[l], g_k_a[l], g_q_m[l], conv_b_w[l], conv_b_b[l],
                  w_rg_a[l], b_rg_a[l], w_rg_i[l], b_rg_i[l], lru_lambda[l], w_out[l],
                  g_ffn[l], w_up[l], conv_f_w[l], conv_f_b[l], w_down[l])
        mem_k, mem_v = memory_kv(mem_prompt, g_mem[l], w_mem_kv[l], g_k_m[l])
        xp, k_a, v_a, bc, bh, fc = trunk_layer(
            xp, functools.partial(band_attention_prompt, rel_table=rel_table[l]),
            mem_k, mem_v,
            jnp.zeros((bp, CONV_B - 1, D_RNN), xp.dtype),
            jnp.zeros((bp, D_RNN), xp.dtype),
            jnp.zeros((bp, CONV_F - 1, 2 * D_FF), xp.dtype),
            *shared)
        ak_p.append(k_a[:, sp - keep:])
        av_p.append(v_a[:, sp - keep:])
        mk_p.append(mem_k)
        mv_p.append(mem_v)
        bc_p.append(bc)
        bh_p.append(bh)
        fc_p.append(fc)
        xs, k_a, v_a, bc, bh, fc = trunk_layer(
            xs, functools.partial(band_attention_sample, k_past=cache_a_k[l],
                                  v_past=cache_a_v[l], rel_table=rel_table[l]),
            cache_mem_k[l], cache_mem_v[l], cache_b_conv[l], state_b_h[l], cache_f_conv[l],
            *shared)
        ak_s.append(k_a)
        av_s.append(v_a)
        bc_s.append(bc)
        bh_s.append(bh)
        fc_s.append(fc)
    return (xp, xs,
            jnp.stack(ak_p), jnp.stack(av_p), jnp.stack(mk_p), jnp.stack(mv_p),
            jnp.stack(bc_p), jnp.stack(bh_p), jnp.stack(fc_p),
            jnp.stack(ak_s), jnp.stack(av_s), jnp.stack(bc_s), jnp.stack(bh_s), jnp.stack(fc_s))


_drawn_inputs = setup_inputs


def setup_inputs(seed=0):
    import zlib

    import numpy as np

    out = dict(_drawn_inputs(seed))
    spreads = {}
    factors = {'g_q_a': 5.729, 'g_q_m': 8.0, 'b_rg_a': 8.0, 'b_rg_i': 8.0, 'conv_f_b': 3.698}
    for name, (base, spread) in spreads.items():
        noise = np.random.default_rng([zlib.crc32(name.encode()), seed]).standard_normal(out[name].shape)
        drawn = base * np.exp(spread * noise) if base else spread * noise
        out[name] = __import__('jax').numpy.asarray(drawn.astype(out[name].dtype))
    for name, factor in factors.items():
        out[name] = (out[name] * factor).astype(out[name].dtype)
    return out
```

```python
from contextlib import ExitStack

import concourse.bass as bass
from concourse import mybir

ALU = mybir.AluOpType
ACT = mybir.ActivationFunctionType
F32 = mybir.dt.float32
F32R = mybir.dt.float32r

P = 128
D = 2048
KT = D // P
SEQ, DEC = 512, 32
ROWS = SEQ + DEC
HALF = ROWS // 2
BODY = SEQ - HALF
N_MEM = 256
HA, HM = 8, 4
D_A, D_M, D_RNN = HA * P, HM * P, 512
RT = D_RNN // P
PAST = 128
D_FF = 6144
FT = D_FF // P
CB, CF = 4, 3
GROUP = 4
NG = FT // GROUP
EPS = 1e-6
MASKED = -1e30
CHUNK = 64
REL = 256
Q_TILES = SEQ // P
TILES = Q_TILES + 1
EXT = 640
PER_H = 3

U_MEM = 0
U_QX = U_MEM + 2 * HM
U_HEAD = U_QX + 2 * HM
U_GB = U_HEAD + 3 * HA
U_OUT = U_GB + RT
U_FF = U_OUT + KT
UP, DOWN = 2 * GROUP, KT * GROUP // 16
FF_PER = UP + DOWN
U_LOOP = U_FF + UP
DOWN_TILES = 16 // GROUP
FF_TILES = UP + KT
U_LAST = U_LOOP + FF_PER * (NG - 1)

PAR = {}
_n = 0
for _name, _w in (("g_attn", KT), ("g_mem", KT), ("g_ffn", KT), ("g_q_a", 1), ("g_k_a", 1),
                  ("g_q_m", 1), ("g_k_m", 1), ("conv_b_w", CB * RT), ("conv_b_b", RT),
                  ("b_rg_a", RT), ("b_rg_i", RT), ("lam", RT), ("h0", RT),
                  ("past_b", (CB - 1) * RT), ("conv_f_w", CF * 2 * FT), ("conv_f_b", 2 * FT),
                  ("past_f", (CF - 1) * 2 * FT)):
    PAR[_name] = _n
    _n += _w
N_PAR = _n

N_MEMROWS = 0
N_MEMK = 1
N_XROWS = N_MEMK + HM
N_QM = N_XROWS + 1
N_HEAD = N_QM + HM
N_X1ROWS = N_HEAD + 2 * HA

W_MEMV = 0
W_M = W_MEMV + HM
PER_M = TILES + 2
W_A = W_M + PER_M * HM
PER_A = 2 + TILES + 2


def tiles_through(u):
    if u < U_LOOP:
        return u + 1
    full, pos = divmod(u - U_LOOP, FF_PER)
    if full == NG - 1:
        own = DOWN_TILES * (pos + 1)
    elif pos < 2:
        own = pos + 1
    elif pos < 2 + DOWN:
        own = 2 + DOWN_TILES * (pos - 1)
    else:
        own = KT + pos - DOWN + 1
    return U_LOOP + FF_TILES * full + own


def encoder(nc, xT, memT, cache_kT, cache_v, cache_mkT, cache_mv, params, rel_table, w_in,
            w_mem_kv, w_rg_a, w_rg_i, w_out, w_up, w_down,
            yT, kT_out, vT_out, mkT_out, mvT_out, b_conv_out, b_h_out, f_conv_out):
    with ExitStack() as ctx:
        def sb(name, shape, dt=F32):
            return ctx.enter_context(nc.sbuf_tensor(name, shape, dt))

        def sem(name):
            return ctx.enter_context(nc.semaphore(name))

        up_w = ROWS + 2 * (CF - 1)
        UP_W = up_w + DEC

        rows = sb("rows", [P, KT, ROWS])
        xh = sb("xh", [P, KT, ROWS], F32R)
        xl = sb("xl", [P, KT, ROWS], F32R)
        raw = sb("raw", [P, 2, 16 * P])
        wh = sb("wh", [P, 2, 16 * P], F32R)
        wl = sb("wl", [P, 2, 16 * P], F32R)
        par = sb("par", [P, N_PAR])
        rstd = sb("rstd", [P, 2, HALF])
        eps = sb("eps", [P, 1])
        zero = sb("zero", [P, 1])
        mean_rows = sb("mean_rows", [P, P])
        f_last = sb("f_last", [P, 2 * FT, 4])
        overlay = nc.sbuf_base

        def place(cursor, name, shape, dt=F32):
            size = 4
            for n in shape[1:]:
                size *= n
            t = nc.alloc_sbuf_tensor_at(name, shape, dt, offset=overlay + cursor[0])
            cursor[0] += -(-size // 32) * 32
            return t

        at = [0]
        ident = place(at, "ident", [P, P])
        mean_head = place(at, "mean_head", [P, P])
        z = place(at, "z", [P, 2, HALF])
        sq = place(at, "sq", [P, 2, HALF])
        sd = place(at, "sd", [P, 2, HALF])
        vT = place(at, "vT", [P, ROWS])
        memk = place(at, "memk", [P, HM, N_MEM])
        memv = place(at, "memv", [P, HM, 2, P])
        qT = place(at, "qT", [P, ROWS])
        kT = place(at, "kT", [P, ROWS])
        v_rows = place(at, "v_rows", [P, TILES, P])
        prob = [place(at, f"prob{t}", [P, max(t + 1, 2) * P]) for t in range(Q_TILES)]
        prob.append(place(at, "prob_s", [P, N_MEM]))
        probT = place(at, "probT", [P, 10 * P + 2 * DEC])
        bias = place(at, "bias", [P, 2, SEQ])
        past = place(at, "past", [P, 2, 4, P])
        rg = place(at, "rg", [P, 2, RT, P])
        xb = place(at, "xb", [P, ROWS + 2 * (CB - 1)])
        scale_q = place(at, "scale_q", [P, 2])
        lam = place(at, "lam", [P, 6, RT])
        neg_b = place(at, "neg_b", [P, 2, RT])
        row_max = place(at, "row_max", [P, TILES])
        row_neg = place(at, "row_neg", [P, TILES])
        row_sum = place(at, "row_sum", [P, TILES])
        row_inv = place(at, "row_inv", [P, TILES])
        b_last = place(at, "b_last", [P, RT, 2 * (CB - 1)])
        h_last = place(at, "h_last", [P, RT, 2])
        assert overlay + at[0] <= nc.sbuf_top, (at, nc.sbuf_top - overlay)
        at_ff = [0]
        hh = place(at_ff, "hh", [P, GROUP, ROWS], F32R)
        hl = place(at_ff, "hl", [P, GROUP, ROWS], F32R)
        upb = [place(at_ff, f"up{n}", [P, UP_W]) for n in range(2)]
        cv = [place(at_ff, f"conv{n}", [P, ROWS + CF - 1]) for n in range(2)]
        sd1 = place(at_ff, "sd1", [P, 2, HALF])
        sum1 = place(at_ff, "sum1", [P, ROWS])
        sq1 = place(at_ff, "sq1", [P, ROWS])
        assert overlay + at_ff[0] <= nc.sbuf_top, (at_ff, nc.sbuf_top - overlay)
        xc, ga, gi, dec, tan = (rows[:, n, :] for n in range(5))
        q_m = [rows[:, 5, :], rows[:, 6, :]]
        sum0, sq0 = qT[:, :], kT[:, :]
        spread, table = probT[0:HA, 0:EXT], probT[0:HA, EXT:EXT + 2 * REL + 1]

        slots = [ctx.enter_context(nc.psum_tensor(f"out{n}", [P, 2, 512], F32)) for n in range(4)]
        scores, flip = slots[2][:, 0, :], slots[2][:, 1, :]
        means = slots[3]

        ext_dram = nc.dram_tensor("bias_by_distance", [HA, EXT], F32, kind="Internal")
        skew_dram = nc.dram_tensor("bias_skewed", [HA, P, SEQ], F32, kind="Internal")

        raw_loaded = [sem("raw_loaded0"), sem("raw_loaded1")]
        hi_split = sem("hi_split")
        lo_split = sem("lo_split")
        tile_ready = sem("tile_ready")
        tile_read = sem("tile_read")
        xhi = sem("xhi")
        xlo = sem("xlo")
        params_in = sem("params_in")
        mem_in = [sem(f"mem_in{n}") for n in range(4)]
        x_in = [sem(f"x_in{n}") for n in range(4)]
        x_again = [sem(f"x_again{n}") for n in range(4)]
        table_in = sem("table_in")
        spread_ready = sem("spread_ready")
        ext_stored = sem("ext_stored")
        skew_stored = sem("skew_stored")
        bias_in = [sem("bias_in0"), sem("bias_in1")]
        bias_masked = sem("bias_masked")
        past_in = [sem("past_in0"), sem("past_in1")]
        rg_zeroed = sem("rg_zeroed")
        gates_in = sem("gates_in")
        consts = sem("consts")
        set_apart = sem("set_apart")
        pool_step = sem("pool_step")
        dve_step = sem("dve_step")
        act_step = sem("act_step")
        sums_ready = sem("sums_ready")
        prepared = sem("prepared")
        lam_exp = sem("lam_exp")
        squares = sem("squares")
        means_ready = sem("means_ready")
        roots_ready = sem("roots_ready")
        normed = sem("normed")
        scores_ready = sem("scores_ready")
        logits_ready = sem("logits_ready")
        exps_ready = sem("exps_ready")
        probs_ready = sem("probs_ready")
        flip_ready = sem("flip_ready")
        flip_read = sem("flip_read")
        k_out = sem("k_out")
        v_out = sem("v_out")
        mk_out = sem("mk_out")
        xb_ready = sem("xb_ready")
        b_tap = sem("b_tap")
        conv_ready = sem("conv_ready")
        gate_ready = sem("gate_ready")
        gate_exp = sem("gate_exp")
        log_ready = sem("log_ready")
        decay_ready = sem("decay_ready")
        ratio_ready = sem("ratio_ready")
        scale_ready = sem("scale_ready")
        g_gelu = sem("g_gelu")
        mixed = sem("mixed")
        edges = sem("edges")
        up_ready = sem("up_ready")
        f_tap = sem("f_tap")
        gate_conv = sem("gate_conv")
        gate_gelu = sem("gate_gelu")
        h_ready = sem("h_ready")
        h_hi = sem("h_hi")
        h_lo = sem("h_lo")
        y_out = sem("y_out")
        small_out = sem("small_out")

        def col(name, n=0):
            if isinstance(n, int):
                return par[:, PAR[name] + n:PAR[name] + n + 1]
            return par[:, bass.ds(n + PAR[name], 1)]

        def halves(ap):
            return ap.rearrange("p (c n) -> p c n", c=2)

        def k_major(w):
            return w.rearrange("(k p) n -> p k n", p=P)

        def flips_before(a):
            return W_M + PER_M * a if a <= HM else W_A + PER_A * (a - HM)

        def keys(a, t):
            if a < HM:
                return N_MEM
            return (t + 1) * P if t < Q_TILES else PAST + DEC

        def probT_at(a, t):
            if a < HM:
                return t * N_MEM
            return t * (t + 1) // 2 * P

        def ff_order(g):
            order = []
            for j in range(GROUP):
                order += [("up", j, 0), ("up", j, 1)]
                if j == 0 and g > 0:
                    order += [("down", q, 0) for q in range(DOWN)]
            return order

        def apart(engine, more):
            if not isinstance(more, int):
                engine.sem_inc(set_apart, 1)

        class Chain:

            def __init__(self, engine, semaphore):
                self.engine, self.semaphore, self.n, self.more = engine, semaphore, 0, 0

            def link(self, instruction):
                self.n += 1
                instruction.then_inc(self.semaphore, 1)
                self.engine.wait_ge(self.semaphore, self.n + self.more)

            def enter(self, i, per):
                self.at, self.per, self.more = self.n, per, per * i

            def leave(self, rounds):
                assert self.n - self.at == self.per, (self.n - self.at, self.per)
                self.n, self.more = self.n + self.per * (rounds - 1), 0

        block = ctx.enter_context(nc.Block())

        @block.sync
        def _(sp):
            def load(u, src, more=0):
                if u >= 2:
                    sp.wait_ge(hi_split, u - 1 + more)
                    sp.wait_ge(lo_split, u - 1 + more)
                    apart(sp, more)
                sp.dma_start(raw[:, u % 2, :].rearrange("p (k n) -> p k n", k=src.shape[1]),
                             src).then_inc(raw_loaded[u % 2], 16)

            def mem_w(c):
                return k_major(w_mem_kv)[:, :, c * P:(c + 1) * P]

            def in_w(c):
                return k_major(w_in)[:, :, bass.ds(c, P)]

            def load_past(a, keys, values):
                n = keys.shape[1] // P
                sp.dma_start(past[:, a % 2, 0:n, :].rearrange("p c n -> p (c n)"),
                             keys).then_inc(past_in[a % 2], 16)
                sp.dma_start(past[:, a % 2, 2:2 + n, :], values).then_inc(past_in[a % 2], 16)

            def m_past(m):
                if m >= 2:
                    sp.wait_ge(flip_ready, flips_before(m - 1))
                load_past(m, cache_mkT[m],
                          cache_mv.rearrange("(c p) h d -> h p c d", p=P)[m])

            def head_loads(h, hr, flips=0, logits=0):
                sp.wait_ge(flip_ready, flips_before(HM + h - 1) + flips)
                if h >= 1:
                    apart(sp, logits)
                    sp.wait_ge(logits_ready, TILES * (HM + h - 1) + logits)
                apart(sp, logits)
                sp.dma_start(bias[:, h % 2, :], skew_dram.ap()[hr] if isinstance(hr, int) else
                             skew_dram.ap()[bass.ds(hr, 1)].rearrange("o p n -> (o p) n")
                             ).then_inc(bias_in[h % 2], 16)
                if isinstance(hr, int):
                    keys, values = cache_kT[hr], cache_v[:, hr, :]
                else:
                    keys = cache_kT[bass.ds(hr, 1)].rearrange("o p n -> (o p) n")
                    values = cache_v[:, bass.ds(hr, 1), :]
                    values = values.rearrange("p o n -> p (o n)")
                load_past(h, keys, values.rearrange("p (c n) -> p c n", c=1))

            def store(dst, h, src, semaphore):
                out = dst[h] if isinstance(h, int) else dst[bass.ds(h, 1)].rearrange("o p n -> (o p) n")
                sp.dma_start(out, src).then_inc(semaphore, 16)

            def store_k(h, hr, more=0):
                sp.wait_ge(normed, N_HEAD + 2 * h + 2 + 2 * more)
                apart(sp, more)
                store(kT_out, hr, kT[:, :], k_out)

            def store_v(h, hr, more=0):
                sp.wait_ge(tile_read, U_HEAD + PER_H * (h + 1) + PER_H * more)
                apart(sp, more)
                store(vT_out, hr, vT[:, :], v_out)

            sp.dma_start(par[:], params).then_inc(params_in, 16)
            for n in range(4):
                sp.dma_start(rows[:, 4 * n:4 * n + 4, 0:N_MEM],
                             k_major(memT)[:, 4 * n:4 * n + 4, :]).then_inc(mem_in[n], 16)
                if n == 0:
                    load(0, mem_w(0))
            load(1, mem_w(1))
            sp.dma_start(table, rel_table).then_inc(table_in, 16)
            load(2, mem_w(2))
            sp.wait_ge(xhi, KT)
            sp.wait_ge(xlo, KT)
            sp.wait_ge(sums_ready, 1)
            for n in range(4):
                sp.dma_start(rows[:, 4 * n:4 * n + 4, :],
                             k_major(xT)[:, 4 * n:4 * n + 4, :]).then_inc(x_in[n], 16)
            load(3, mem_w(3))
            sp.wait_ge(spread_ready, 1)
            sp.dma_start(ext_dram.ap(), spread).then_inc(ext_stored, 16)
            load(4, mem_w(4))
            sp.wait_ge(rg_zeroed, 1)
            for g, w in enumerate((w_rg_a, w_rg_i)):
                for b in range(2):
                    half = slice(CHUNK * b, CHUNK * (b + 1))
                    sp.dma_start(rg[half, g, :, half],
                                 w.rearrange("(t b) i j -> b i t j", b=2)[b]).then_inc(gates_in, 16)
            load(5, mem_w(5))
            sp.wait_ge(ext_stored, 16)
            sp.dma_start(skew_dram.ap(), bass.AP(ext_dram, P - 1, [[EXT, HA], [-1, P], [1, SEQ]])
                         ).then_inc(skew_stored, 16)
            load(6, mem_w(6))
            for n in range(HM):
                if n < 3:
                    sp.wait_ge(normed, N_MEMK + n + 1)
                    sp.dma_start(mkT_out[n], memk[:, n, :]).then_inc(mk_out, 16)
            load(7, mem_w(7))
            sp.wait_ge(normed, N_MEMK + HM)
            sp.dma_start(mkT_out[HM - 1], memk[:, HM - 1, :]).then_inc(mk_out, 16)
            for m in range(HM):
                for n in range(2):
                    load(U_QX + 2 * m + n, in_w(3 * D_A + n * D_M + m * P))
                    if m < 2:
                        sp.wait_ge(tile_read, HM + 2 * m + n + 1)
                        sp.dma_start(mvT_out[2 * m + n], vT[:, 0:N_MEM]).then_inc(v_out, 16)
                if m >= 1:
                    m_past(m - 1)
            sp.wait_ge(skew_stored, 16)

            def period(h, hr, i=0):
                u, more = U_HEAD + PER_H * h, 2 * PER_H * i
                load(u, in_w(hr * P), more)
                if h >= 1:
                    head_loads(h - 1, hr - 1, 2 * PER_A * i, 2 * TILES * i)
                if h >= 2:
                    store_v(h - 2, hr - 2, 2 * i)
                load(u + 1, in_w(hr * P + D_A), more)
                if h == 0:
                    m_past(HM - 1)
                load(u + 2, in_w(hr * P + 2 * D_A), more)
                if h >= 1:
                    store_k(h - 1, hr - 1, 2 * i)

            period(0, 0)
            period(1, 1)
            with sp.Fori(0, 3) as i:
                period(2, 2 * i + 2, i)
                period(3, 2 * i + 3, i)
            load(U_GB, in_w(3 * D_A + D_M + D_RNN))
            head_loads(HA - 1, HA - 1)
            store_v(HA - 2, HA - 2)
            load(U_GB + 1, in_w(3 * D_A + D_M + D_RNN + P))
            load(U_GB + 2, in_w(3 * D_A + D_M + D_RNN + 2 * P))
            store_k(HA - 1, HA - 1)
            load(U_GB + 3, in_w(3 * D_A + D_M + D_RNN + 3 * P))
            store_v(HA - 1, HA - 1)

            def out_w(m):
                return k_major(w_out)[:, :, bass.ds(m * P, P)]

            load(U_OUT, out_w(0))
            load(U_OUT + 1, out_w(1))
            sp.wait_ge(mixed, RT)
            sp.dma_start(b_conv_out, b_last[:]).then_inc(small_out, 16)
            sp.dma_start(b_h_out, h_last[:]).then_inc(small_out, 16)
            sp.wait_ge(xhi, 3 * KT)
            sp.wait_ge(xlo, 3 * KT)
            for n in range(4):
                sp.dma_start(rows[:, 4 * n:4 * n + 4, :],
                             k_major(xT)[:, 4 * n:4 * n + 4, :]).then_inc(x_again[n], 16)
            load(U_OUT + 2, out_w(2))
            load(U_OUT + 3, out_w(3))
            with sp.Fori(0, 3) as i:
                for n in range(4):
                    load(U_OUT + 4 + n, out_w(4 * i + 4 + n), 4 * i)

            def up_w(g, j, gate):
                return k_major(w_up)[:, :, bass.ds((g * GROUP + j) * P + gate * D_FF, P)]

            def down_w(g, q):
                n = DOWN_TILES * P
                return k_major(w_down)[:, bass.ds(g * GROUP, GROUP), q * n:(q + 1) * n]

            for j in range(GROUP):
                load(U_FF + 2 * j, up_w(0, j, 0))
                load(U_FF + 2 * j + 1, up_w(0, j, 1))
            with sp.Fori(0, NG - 1) as i:
                u = U_LOOP
                for j in range(GROUP):
                    for gate in range(2):
                        load(u, up_w(i + 1, j, gate), FF_PER * i)
                        u += 1
                    if j == 0:
                        for q in range(DOWN):
                            load(u, down_w(i, q), FF_PER * i)
                            u += 1
            for q in range(DOWN):
                load(U_LAST + q, down_w(NG - 1, q))
            sp.wait_ge(up_ready, 2 * FT)
            sp.dma_start(f_conv_out, f_last[:]).then_inc(small_out, 16)
            for q in range(DOWN):
                sp.wait_ge(tile_read, tiles_through(U_LAST + q))
                n = slice(DOWN_TILES * q, DOWN_TILES * (q + 1))
                sp.dma_start(k_major(yT)[:, n, :], rows[:, n, :]).then_inc(y_out, 16)
            sp.wait_ge(mk_out, 16 * HM)
            sp.wait_ge(k_out, 16 * HA)
            sp.wait_ge(v_out, 16 * (HM + HA))
            sp.wait_ge(small_out, 16 * 3)
            sp.wait_ge(y_out, 16 * DOWN)

        @block.gpsimd
        def _(pool):
            chain = Chain(pool, pool_step)
            nc.gpsimd.memset(mean_rows[:], 1.0 / D).then_inc(consts, 1)
            nc.gpsimd.memset(mean_head[:], 1.0 / P).then_inc(consts, 1)
            nc.gpsimd.memset(eps[:], EPS).then_inc(consts, 1)
            nc.gpsimd.memset(zero[:], 0.0).then_inc(consts, 1)
            chain.link(nc.gpsimd.memset(ident[:], 0.0))
            nc.gpsimd.affine_select(out=ident[:], in_=ident[:], compare_op=ALU.not_equal, fill=1.0,
                                    base=0, pattern=[[-1, P]], channel_multiplier=1
                                    ).then_inc(consts, 1)
            nc.gpsimd.memset(rg[:], 0.0).then_inc(rg_zeroed, 1)
            nc.gpsimd.memset(xb[:, 0:CB - 1], 0.0).then_inc(consts, 1)

            def sum_squares(total, square, width, ready):
                for k in range(KT):
                    ready(k)
                    tile = rows[:, k, 0:width]
                    if k == 0:
                        chain.link(nc.gpsimd.tensor_tensor(total[:, 0:width], tile, tile, ALU.mult))
                        continue
                    chain.link(nc.gpsimd.tensor_tensor(square[:, 0:width], tile, tile, ALU.mult))
                    add = nc.gpsimd.tensor_tensor(total[:, 0:width], total[:, 0:width],
                                                  square[:, 0:width], ALU.add)
                    if k < KT - 1:
                        chain.link(add)
                add.then_inc(sums_ready, 1)

            sum_squares(sum0, sq0, N_MEM, lambda k: pool.wait_ge(mem_in[k // 4], 16))
            pool.wait_ge(sums_ready, 1)
            pool.wait_ge(means_ready, N_MEMROWS + 1)
            sum_squares(sum0, sq0, ROWS, lambda k: pool.wait_ge(x_in[k // 4], 16))

            def mask(h, i=0):
                pool.wait_ge(bias_in[h % 2], 16 * (h // 2 + 1) + 16 * i)
                apart(pool, i)
                nc.gpsimd.memset(bias[0:CHUNK, h % 2, SEQ - CHUNK:SEQ], MASKED).then_inc(bias_masked, 1)

            mask(0)
            with pool.Fori(0, 3) as i:
                mask(1, i)
                mask(2, i)
            mask(HA - 1)

            pool.wait_ge(flip_read, flips_before(HM + HA))
            pool.wait_ge(mixed, RT)
            pool.wait_ge(k_out, 16 * HA)
            pool.wait_ge(v_out, 16 * (HM + HA))
            pool.wait_ge(xlo, 3 * KT)
            sum_squares(sum1, sq1, ROWS, lambda k: pool.wait_ge(tile_read, U_OUT + k + 1))
            for n in range(2):
                nc.gpsimd.memset(upb[n][:, 0:CF - 1], 0.0).then_inc(edges, 1)

        @block.scalar
        def _(act):
            def hi(u, more=0, tiles=0):
                if u:
                    act.wait_ge(hi_split, u + more)
                act.wait_ge(raw_loaded[u % 2], 16 * (u // 2 + 1) + 8 * more)
                if u >= 2:
                    act.wait_ge(tile_ready, tiles_through(u - 2) + tiles)
                nc.scalar.copy(wh[:, u % 2, :], raw[:, u % 2, :]).then_inc(hi_split, 1)

            def split_rows(gain, width, ready, between=None):
                for k in range(KT):
                    ready(k)
                    src, dst = rows[:, k, 0:width], xh[:, k, 0:width]
                    if gain is None:
                        nc.scalar.copy(dst, src).then_inc(xhi, 1)
                    else:
                        nc.scalar.mul(dst, src, col(gain, k)).then_inc(xhi, 1)
                    if between and k == 11:
                        between()

            def square(n, u, more=0, tiles=0, width=ROWS):
                act.wait_ge(tile_read, u + 1 + tiles)
                act.wait_ge(means_ready, n + more)
                src, dst = (z[:], sq[:]) if width == ROWS else (z[:, 0, 0:width], sq[:, 0, 0:width])
                nc.scalar.activation(dst, src, ACT.Square).then_inc(squares, 1)

            def root(n, more=0, width=ROWS, out=sd):
                act.wait_ge(means_ready, n + 1 + more)
                if n > 0:
                    act.wait_ge(normed, n + more)
                if width == ROWS:
                    dst, src = out[:], means[:, :, 0:HALF]
                else:
                    dst, src = out[:, 0, 0:width], means[:, 0, 0:width]
                nc.scalar.activation(dst, src, ACT.Sqrt, bias=eps[:]).then_inc(roots_ready, 1)

            def exps(a, t, more=0):
                act.wait_ge(logits_ready, TILES * a + t + 1 + TILES * more)
                n, w = (P if t < Q_TILES else DEC), keys(a, t)
                nc.scalar.activation(prob[t][0:n, 0:w], prob[t][0:n, 0:w], ACT.Exp,
                                     bias=row_neg[0:n, t:t + 1],
                                     accum_out=row_sum[0:n, t:t + 1]).then_inc(exps_ready, 1)

            def read_prob(a, t, more=0):
                w = flips_before(a) + (2 if a >= HM else 0) + t
                act.wait_ge(flip_ready, w + 1 + PER_A * more)
                at = probT_at(a, t)
                if t < Q_TILES:
                    n = keys(a, t)
                    nc.scalar.copy(probT[:, at:at + n], flip[:, 0:n]).then_inc(flip_read, 1)
                elif a < HM:
                    nc.scalar.copy(probT[:, at:at + 2 * DEC], flip[:, 0:2 * DEC]).then_inc(flip_read, 1)
                else:
                    chain.link(nc.scalar.copy(probT[:, at:at + DEC], flip[:, 0:DEC]))
                    nc.scalar.copy(probT[0:DEC, at + DEC:at + 2 * DEC],
                                   flip[0:DEC, DEC:2 * DEC]).then_inc(flip_read, 1)

            def read_v(h, s, more=0):
                act.wait_ge(flip_ready, flips_before(HM + h) + s + 1 + PER_A * more)
                if s == 0:
                    nc.scalar.copy(v_rows[:, 0:Q_TILES, :],
                                   flip.rearrange("p (t n) -> p t n", n=P)).then_inc(flip_read, 1)
                else:
                    nc.scalar.copy(v_rows[0:DEC, Q_TILES, :], flip[0:DEC, 0:P]).then_inc(flip_read, 1)

            def read_output(a, s, slot, more=0):
                w = flips_before(a + 1) - 2 + s
                act.wait_ge(flip_ready, w + 1 + PER_A * more)
                n, at = (SEQ, 0) if s == 0 else (DEC, SEQ)
                dst = rows[:, slot, at:at + n] if isinstance(slot, int) else \
                    rows[:, bass.ds(slot, 1), at:at + n].rearrange("p o n -> p (o n)")
                nc.scalar.copy(dst, flip[:, 0:n]).then_inc(flip_read, 1)

            def memory_head(m, beat):
                if beat == 8:
                    read_output(m, 1, HA + m)
                if beat == 7:
                    read_output(m, 0, HA + m)
                if 2 <= beat < 2 + TILES:
                    read_prob(m, beat - 2)
                if beat < TILES:
                    exps(m, beat)

            def band_head(h, hr, beat, i=0):
                a = HM + h
                if beat in (1, 2):
                    read_v(h, beat - 1, 2 * i)
                if 3 <= beat < 3 + TILES:
                    read_prob(a, beat - 3, 2 * i)
                if beat in (8, 9):
                    read_output(a, beat - 8, hr, 2 * i)
                if beat < TILES:
                    exps(a, beat, 2 * i)

            def recurrence(j, beat):
                if beat == 0:
                    act.wait_ge(xb_ready, j + 1)
                    w, b = col("conv_b_w", (CB - 1) * RT + j), col("conv_b_b", j)
                    chain.link(nc.scalar.activation(xc[:, 0:SEQ], xb[:, CB - 1:CB - 1 + SEQ],
                                                    ACT.Identity, bias=b, scale=w))
                    at = SEQ + 2 * (CB - 1)
                    nc.scalar.activation(xc[:, SEQ:ROWS], xb[:, at:at + DEC], ACT.Identity,
                                         bias=b, scale=w).then_inc(b_tap, 1)
                if beat in (2, 3):
                    n = beat - 2
                    act.wait_ge(gate_ready, 2 * j + n + 1)
                    nc.scalar.activation(halves((ga, gi)[n]), means[:, :, 0:HALF], ACT.Exp,
                                         bias=neg_b[:, n, j:j + 1], scale=-1.0).then_inc(gate_exp, 1)
                if beat == 4:
                    act.wait_ge(log_ready, j + 1)
                    chain.link(nc.scalar.activation(dec, ga, ACT.Exp, scale=-1.0))
                    nc.scalar.activation(tan, ga, ACT.Tanh).then_inc(decay_ready, 1)
                if beat == 5:
                    act.wait_ge(ratio_ready, j + 1)
                    nc.scalar.activation(tan, tan, ACT.Sqrt, bias=zero[:]).then_inc(scale_ready, 1)

            def head_norm(beat, h, q_or_k, i=0):
                n = N_HEAD + 2 * h + q_or_k
                if beat == 0:
                    square(n, U_HEAD + PER_H * h + q_or_k, 4 * i, 2 * PER_H * i)
                else:
                    root(n, 4 * i)

            chain = Chain(act, act_step)
            act.wait_ge(consts, 6)
            hi(0)
            act.wait_ge(params_in, 16)
            split_rows("g_mem", N_MEM, lambda k: act.wait_ge(mem_in[k // 4], 16))
            hi(1)
            act.wait_ge(prepared, 1)
            nc.scalar.activation(lam[:, 1, :], lam[:, 0, :], ACT.Exp, scale=-1.0).then_inc(lam_exp, 1)
            root(N_MEMROWS, width=N_MEM)
            for u in range(1, U_QX):
                hi(u + 1)
                if u <= HM:
                    square(N_MEMK + u - 1, u - 1, width=N_MEM)
                    root(N_MEMK + u - 1, width=N_MEM)
                else:
                    m = u - HM - 1
                    act.wait_ge(flip_ready, m + 1)
                    nc.scalar.copy(memv[:, m], flip[:, 0:N_MEM].rearrange("p (c n) -> p c n", c=2)
                                   ).then_inc(flip_read, 1)

            def x_ready(k):
                act.wait_ge(x_in[k // 4], 16)
                if k == 0:
                    act.wait_ge(tile_ready, U_QX)

            split_rows("g_attn", ROWS, x_ready, lambda: hi(U_QX + 1))
            act.wait_ge(flip_ready, HM)
            nc.scalar.copy(memv[:, HM - 1], flip[:, 0:N_MEM].rearrange("p (c n) -> p c n", c=2)
                           ).then_inc(flip_read, 1)
            root(N_XROWS)
            for m in range(HM):
                u = U_QX + 2 * m
                if m >= 1:
                    hi(u + 1)
                    for beat in range(4):
                        if beat == 0 and m >= 2:
                            memory_head(m - 2, 8)
                        recurrence(m - 1, beat)
                        memory_head(m - 1, beat)
                hi(u + 2)
                square(N_QM + m, u)
                for beat in range(4, 8):
                    if beat == 5:
                        root(N_QM + m)
                    if m >= 1:
                        recurrence(m - 1, beat)
                        memory_head(m - 1, beat)

            for beat in range(12):
                if beat % 4 == 0:
                    hi(U_HEAD + 1 + beat // 4)
                if beat == 0:
                    memory_head(HM - 2, 8)
                if beat in (4, 8):
                    head_norm(0, 0, beat // 4 - 1)
                if beat in (5, 9):
                    head_norm(1, 0, beat // 4 - 1)
                if beat < 9:
                    recurrence(HM - 1, beat)
                    memory_head(HM - 1, beat)

            def period(h, hr, i=0):
                u, more = U_HEAD + PER_H * h, 2 * PER_H * i
                for beat in range(12):
                    if beat % 4 == 0:
                        hi(u + 1 + beat // 4, more, more)
                    if beat in (4, 8):
                        head_norm(0, h, beat // 4 - 1, i)
                    if beat in (5, 9):
                        head_norm(1, h, beat // 4 - 1, i)
                    band_head(h - 1, hr - 1, beat, i)

            period(1, 1)
            with act.Fori(0, 3) as i:
                chain.enter(i, 2)
                period(2, 2 * i + 2, i)
                period(3, 2 * i + 3, i)
                chain.leave(3)

            def gelu_gate(j):
                act.wait_ge(tile_read, U_GB + j + 1)
                nc.scalar.activation(z[:], z[:], ACT.Gelu_apprx_tanh).then_inc(g_gelu, 1)

            for beat in range(12):
                if beat % 4 == 0:
                    hi(U_GB + 1 + beat // 4)
                band_head(HA - 1, HA - 1, beat)
                if beat in (7, 11):
                    gelu_gate(beat // 4 - 1)
            hi(U_OUT)
            gelu_gate(2)
            gelu_gate(3)

            def o_ready(k):
                if k == 0:
                    act.wait_ge(tile_ready, U_OUT)
                    act.wait_ge(flip_read, flips_before(HM + HA))
                if k >= HA + HM:
                    act.wait_ge(mixed, k - HA - HM + 1)

            split_rows(None, ROWS, o_ready, lambda: hi(U_OUT + 1))
            for n in range(1, 4):
                hi(U_OUT + n + 1)
            with act.Fori(0, 2) as i:
                for n in range(4):
                    hi(U_OUT + 5 + n, 4 * i, 4 * i)
            for u in range(U_OUT + 13, U_FF + 1):
                hi(u)

            def x1_ready(k):
                act.wait_ge(tile_read, U_OUT + k + 1)
                if k == 0:
                    act.wait_ge(tile_ready, U_FF)

            split_rows("g_ffn", ROWS, x1_ready, lambda: hi(U_FF + 1))
            root(N_X1ROWS, out=sd1)

            def feed(g0, i=0, gr=0):
                order = ff_order(g0)
                u = U_FF if g0 == 0 else U_LOOP
                for pos, (kind, j, gate) in enumerate(order):
                    if not (g0 == 0 and pos == 0):
                        hi_next(u + pos, g0, i)
                    last = order[pos - 1] if pos else ("up", GROUP - 1, 1)
                    if pos or g0:
                        gg, ii = (g0, i) if pos else (g0 - 1, i)
                        up_tile(gg, ii, gr if pos else gr - 1, last, pos == 2 and g0)
                    if g0 and pos == 2 + DOWN:
                        write_h(g0, i, 0)

            def hi_next(u, g0, i):
                hi(u + 1, FF_PER * i, FF_TILES * i)

            def up_tile(g, i, gr, unit, held):
                kind, j, gate = unit
                if kind == "down":
                    return
                e = 2 * GROUP * g + 2 * j + gate
                act.wait_ge(up_ready, e + 1 + 2 * GROUP * i)
                done = GROUP * g + j
                if done or not isinstance(i, int):
                    act.wait_ge(h_ready if gate else h_lo, done + GROUP * i)
                tile = gate * FT + GROUP * gr + j
                nc.scalar.activation(cv[gate][:], upb[gate][:, CF - 1:up_w], ACT.Identity,
                                     bias=col("conv_f_b", tile),
                                     scale=col("conv_f_w", tile + (CF - 1) * 2 * FT)
                                     ).then_inc(f_tap, 1)
                if gate:
                    act.wait_ge(gate_conv, done + 1 + GROUP * i)
                    nc.scalar.activation(cv[1][:], cv[1][:], ACT.Gelu_apprx_tanh).then_inc(gate_gelu, 1)
                    if not held:
                        write_h(g, i, j)

            def write_h(g, i, j):
                act.wait_ge(h_ready, GROUP * g + j + 1 + GROUP * i)
                if g:
                    act.wait_ge(tile_ready, tiles_through(U_LOOP + 1 + DOWN + FF_PER * (g - 1))
                                + FF_TILES * i)
                chain.link(nc.scalar.copy(hh[:, j, 0:SEQ], cv[0][:, 0:SEQ]))
                nc.scalar.copy(hh[:, j, SEQ:ROWS], cv[0][:, SEQ + CF - 1:]).then_inc(h_hi, 1)

            feed(0)
            with act.Fori(0, NG - 1) as i:
                chain.enter(i, GROUP)
                feed(1, i, i + 1)
                chain.leave(NG - 1)
            last = (U_LAST, NG - 1)
            hi(U_LAST + 1)
            up_tile(NG - 1, 0, NG - 1, ("up", GROUP - 1, 1), False)
            for q in range(1, DOWN - 1):
                hi(U_LAST + q + 1)

        @block.vector
        def _(dve):
            chain = Chain(dve, dve_step)
            link = chain.link

            def lo(u, more=0):
                if u:
                    dve.wait_ge(lo_split, u + more)
                dve.wait_ge(hi_split, u + 1 + more)
                nc.vector.tensor_tensor(wl[:, u % 2, :], raw[:, u % 2, :],
                                        wh[:, u % 2, :].bitcast(F32), ALU.subtract).then_inc(lo_split, 1)

            def split_rows(first, gain, width, between=None):
                for k in range(KT):
                    dve.wait_ge(xhi, first + k + 1)
                    src, high, dst = (t[:, k, 0:width] for t in (rows, xh, xl))
                    if gain is None:
                        ins = nc.vector.tensor_tensor(dst, src, high.bitcast(F32), ALU.subtract)
                    else:
                        ins = nc.vector.scalar_tensor_tensor(dst, src, col(gain, k), high.bitcast(F32),
                                                             ALU.mult, ALU.subtract)
                    ins.then_inc(xlo, 1)
                    if between and k == 11:
                        between()

            def psum(t):
                return slots[t % 2][:, :, 0:HALF]

            def read_z(u, n, more=0, norms=0, width=ROWS):
                dve.wait_ge(normed, n + norms)
                dve.wait_ge(tile_ready, u + 1 + more)
                if width == ROWS:
                    dst, src, r = z[:], psum(u), rstd[:]
                else:
                    dst, src, r = z[:, 0, 0:width], psum(u)[:, 0, 0:width], rstd[:, 0, 0:width]
                nc.vector.tensor_tensor(dst, src, r, ALU.mult).then_inc(tile_read, 1)

            def read_v(u, v, more=0, more_v=0, width=ROWS):
                if v:
                    dve.wait_ge(v_out, 16 * v + 16 * more_v)
                    flips = v if v <= HM else flips_before(v - 1) + 2
                    dve.wait_ge(flip_ready, flips + PER_A * more_v)
                dve.wait_ge(tile_ready, u + 1 + more)
                if width == ROWS:
                    dst, src, r = halves(vT[:, :]), psum(u), rstd[:]
                else:
                    dst, src, r = vT[:, 0:width], psum(u)[:, 0, 0:width], rstd[:, 0, 0:width]
                nc.vector.tensor_tensor(dst, src, r, ALU.mult).then_inc(tile_read, 1)

            def normalise(n, dst, gain, more=0, width=ROWS):
                dve.wait_ge(roots_ready, n + 1 + more)
                if width == ROWS:
                    r, src = sd[:], z[:]
                    dst = halves(dst)
                else:
                    r, src = sd[:, 0, 0:width], z[:, 0, 0:width]
                link(nc.vector.reciprocal(r, r))
                nc.vector.scalar_tensor_tensor(dst, src, gain, r, ALU.mult, ALU.mult).then_inc(normed, 1)

            def row_factor(n, src, width=ROWS):
                dve.wait_ge(roots_ready, n + 1)
                dst, src = (rstd[:], src[:]) if width == ROWS else \
                    (rstd[:, 0, 0:width], src[:, 0, 0:width])
                nc.vector.reciprocal(dst, src).then_inc(normed, 1)
                dve.wait_ge(normed, n + 1)

            def logits(a, t, more=0):
                n, w = (P if t < Q_TILES else DEC), keys(a, t)
                dve.wait_ge(scores_ready, TILES * a + t + 1 + TILES * more)
                if a >= 1:
                    before = flips_before(a - 1) + (2 if a > HM else 0) + t + 1
                    dve.wait_ge(flip_ready, before + PER_A * more)
                if a < HM:
                    add = zero[0:n, 0:1].to_broadcast([n, w])
                else:
                    h = a - HM
                    if t == 0:
                        dve.wait_ge(bias_masked, h + 1 + more)
                    first = SEQ - w if t < Q_TILES else Q_TILES * P - PAST - P
                    add = bias[0:n, h % 2, first:first + w]
                apart(dve, more)
                link(nc.vector.tensor_tensor_reduce(
                    out=prob[t][0:n, 0:w], in0=scores[0:n, 0:w], in1=add, scale=1.0, scalar=-3e38,
                    op0=ALU.add, op1=ALU.max, accum_out=row_max[0:n, t:t + 1]))
                nc.vector.tensor_scalar(row_neg[0:n, t:t + 1], row_max[0:n, t:t + 1], -1.0, None,
                                        ALU.mult).then_inc(logits_ready, 1)

            def probs(a, t, more=0):
                n, w = (P if t < Q_TILES else DEC), keys(a, t)
                dve.wait_ge(exps_ready, TILES * a + t + 1 + TILES * more)
                link(nc.vector.reciprocal(row_inv[0:n, t:t + 1], row_sum[0:n, t:t + 1]))
                nc.vector.tensor_scalar(prob[t][0:n, 0:w], prob[t][0:n, 0:w], row_inv[0:n, t:t + 1],
                                        None, ALU.mult).then_inc(probs_ready, 1)

            def head(a, beat, more=0):
                if beat < TILES:
                    logits(a, beat, more)
                if 1 <= beat <= TILES:
                    probs(a, beat - 1, more)

            def split_pieces(ap, first, gap):
                body = ap[:, first:first + ROWS].rearrange("p (c n) -> p c n", c=2)[:, :, 0:BODY]
                w = HALF + gap
                at = first + BODY
                tail = ap[:, at:at + w + DEC]
                return body, tail, w

            def recurrence(j, beat):
                def tap(k):
                    return col("conv_b_w", k * RT + j)

                if beat == 0:
                    u = U_QX + 2 * j + 1
                    dve.wait_ge(tile_ready, u + 1)
                    src = psum(u)
                    nc.vector.tensor_tensor(
                        xb[:, CB - 1:CB - 1 + HALF], src[:, 0, :], rstd[:, 0, :], ALU.mult)
                    nc.vector.tensor_tensor(
                        xb[:, CB - 1 + HALF:CB - 1 + SEQ], src[:, 1, 0:BODY], rstd[:, 1, 0:BODY], ALU.mult)
                    at = SEQ + 2 * (CB - 1)
                    nc.vector.tensor_tensor(xb[:, at:at + DEC], src[:, 1, BODY:HALF],
                                            rstd[:, 1, BODY:HALF], ALU.mult).then_inc(tile_read, 1)
                    dve.wait_ge(tile_read, u + 1)
                    past_b = par[:, PAR["past_b"] + j * (CB - 1):PAR["past_b"] + (j + 1) * (CB - 1)]
                    nc.vector.tensor_copy(xb[:, SEQ + CB - 1:at], past_b)
                    nc.vector.tensor_copy(b_last[:, j, 0:CB - 1], xb[:, SEQ:SEQ + CB - 1])
                    nc.vector.tensor_copy(b_last[:, j, CB - 1:], xb[:, at + DEC - CB + 1:at + DEC]
                                          ).then_inc(xb_ready, 1)
                if beat == 1:
                    dve.wait_ge(b_tap, j + 1)
                    dve.wait_ge(xb_ready, j + 1)
                    for k in range(CB - 2, -1, -1):
                        at = SEQ + CB - 1 + k
                        nc.vector.scalar_tensor_tensor(xc[:, 0:SEQ], xb[:, k:k + SEQ], tap(k),
                                                       xc[:, 0:SEQ], ALU.mult, ALU.add)
                        ins = nc.vector.scalar_tensor_tensor(xc[:, SEQ:ROWS], xb[:, at:at + DEC],
                                                             tap(k), xc[:, SEQ:ROWS], ALU.mult, ALU.add)
                        if k:
                            link(ins)
                    ins.then_inc(conv_ready, 1)
                if beat == 3:
                    dve.wait_ge(gate_exp, 2 * j + 1)
                    link(nc.vector.tensor_scalar(ga, ga, 1.0, None, ALU.add))
                    link(nc.vector.reciprocal(ga, ga))
                    nc.vector.tensor_scalar(ga, ga, lam[:, 0, j:j + 1], None, ALU.mult).then_inc(log_ready, 1)
                if beat == 4:
                    dve.wait_ge(gate_exp, 2 * j + 2)
                    link(nc.vector.tensor_scalar(gi, gi, 1.0, None, ALU.add))
                    link(nc.vector.reciprocal(gi, gi))
                    link(nc.vector.tensor_tensor(gi, gi, xc, ALU.mult))
                if beat == 5:
                    dve.wait_ge(decay_ready, j + 1)
                    link(nc.vector.tensor_scalar(ga, tan, 1.0, None, ALU.add))
                    link(nc.vector.reciprocal(ga, ga))
                    nc.vector.scalar_tensor_tensor(tan, tan, 2.0, ga, ALU.mult, ALU.mult
                                                   ).then_inc(ratio_ready, 1)
                if beat == 6:
                    dve.wait_ge(scale_ready, j + 1)
                    link(nc.vector.tensor_tensor(gi, gi, tan, ALU.mult))
                    out = rows[:, HA + HM + j, :]
                    nc.vector.tensor_tensor_scan(out[:, 0:SEQ], dec[:, 0:SEQ], gi[:, 0:SEQ], 0.0,
                                                 ALU.mult, ALU.add)
                    link(nc.vector.tensor_tensor_scan(out[:, SEQ:ROWS], dec[:, SEQ:ROWS],
                                                      gi[:, SEQ:ROWS], col("h0", j), ALU.mult, ALU.add))
                    nc.vector.tensor_copy(h_last[:, j, 0:1], out[:, SEQ - 1:SEQ])
                    link(nc.vector.tensor_copy(h_last[:, j, 1:2], out[:, ROWS - 1:ROWS]))

            dve.wait_ge(consts, 6)
            dve.wait_ge(params_in, 16)
            v = nc.vector
            raw_lam = par[:, PAR["lam"]:PAR["lam"] + RT]
            L = [lam[:, n, :] for n in range(6)]
            link(v.tensor_scalar(L[2], raw_lam, -1.0, None, ALU.mult))
            link(v.tensor_tensor(L[0], L[2], raw_lam, ALU.max))
            v.tensor_scalar(L[2], L[2], 0.0, None, ALU.max)
            v.tensor_scalar(neg_b[:, 0, :], par[:, PAR["b_rg_a"]:PAR["b_rg_a"] + RT], -1.0, None, ALU.mult)
            v.tensor_scalar(neg_b[:, 1, :], par[:, PAR["b_rg_i"]:PAR["b_rg_i"] + RT], -1.0, None, ALU.mult)
            v.tensor_scalar(scale_q[:, 0:1], col("g_q_a"), P ** -0.5, None, ALU.mult)
            v.tensor_scalar(scale_q[:, 1:2], col("g_q_m"), P ** -0.5, None, ALU.mult).then_inc(prepared, 1)

            lo(0)
            split_rows(0, "g_mem", N_MEM)
            lo(1)
            dve.wait_ge(lam_exp, 1)
            link(v.tensor_scalar(L[3], L[1], 2.0, None, ALU.add))
            link(v.reciprocal(L[3], L[3]))
            link(v.tensor_tensor(L[4], L[1], L[3], ALU.mult))
            link(v.tensor_tensor(L[5], L[4], L[4], ALU.mult))
            link(v.tensor_scalar(L[3], L[5], 1.0 / 15, 1.0 / 13, ALU.mult, ALU.add))
            for n in (11, 9, 7, 5, 3, 1):
                link(v.tensor_tensor(L[3], L[3], L[5], ALU.mult))
                link(v.tensor_scalar(L[3], L[3], 1.0 / n, None, ALU.add))
            link(v.tensor_tensor(L[3], L[3], L[4], ALU.mult))
            link(v.scalar_tensor_tensor(L[3], L[3], 2.0, L[2], ALU.mult, ALU.add))
            link(v.tensor_scalar(L[0], L[3], 8.0, None, ALU.mult))
            dve.wait_ge(table_in, 16)
            flat = Q_TILES * P - 1 - REL
            v.tensor_copy(spread[:, 0:flat], table[:, 2 * REL:2 * REL + 1].to_broadcast([HA, flat]))
            v.tensor_copy(spread[:, flat:EXT], table[:, 2 * REL:2 * REL - (EXT - flat):-1]
                          ).then_inc(spread_ready, 1)

            row_factor(N_MEMROWS, sd, N_MEM)
            for u in range(1, U_QX):
                lo(u + 1)
                if u <= HM:
                    read_z(u - 1, N_MEMK + u - 1, width=N_MEM)
                    normalise(N_MEMK + u - 1, memk[:, u - 1, :], col("g_k_m"), width=N_MEM)
                else:
                    read_v(u - 1, u - 1 - HM, width=N_MEM)
            split_rows(KT, "g_attn", ROWS, lambda: lo(U_QX + 1))
            read_v(U_QX - 1, HM - 1, width=N_MEM)
            row_factor(N_XROWS, sd)
            for m in range(HM):
                u = U_QX + 2 * m
                if m >= 1:
                    lo(u + 1)
                    for beat in range(4):
                        recurrence(m - 1, beat)
                        head(m - 1, beat)
                lo(u + 2)
                read_z(u, N_QM + m)
                for beat in range(4, 8):
                    if beat == 6:
                        normalise(N_QM + m, q_m[m % 2], scale_q[:, 1:2])
                    if m >= 1:
                        recurrence(m - 1, beat)
                        head(m - 1, beat)

            def period(h, i=0):
                u, more, a = U_HEAD + PER_H * h, 2 * PER_H * i, HM + h - 1
                for beat in range(12):
                    if beat % 4 == 0:
                        lo(u + 1 + beat // 4, more)
                    if beat == 0 and h >= 1:
                        read_v(u - 1, HM + h - 1, more, 2 * i)
                    if beat in (4, 8):
                        read_z(u + beat // 4 - 1, N_HEAD + 2 * h + beat // 4 - 1, more, 4 * i)
                    if beat == 6:
                        dve.wait_ge(scores_ready, TILES * (a + 1) + 2 * TILES * i)
                        normalise(N_HEAD + 2 * h, qT[:, :], scale_q[:, 0:1], 4 * i)
                    if beat == 10:
                        if h >= 1:
                            dve.wait_ge(k_out, 16 * h + 32 * i)
                        normalise(N_HEAD + 2 * h + 1, kT[:, :], col("g_k_a"), 4 * i)
                    if h == 0:
                        recurrence(HM - 1, beat)
                    head(a, beat, 2 * i)

            period(0)
            period(1)
            with dve.Fori(0, 3) as i:
                chain.enter(i, 24)
                period(2, i)
                period(3, i)
                chain.leave(3)

            def read_g(j):
                if j == 0:
                    dve.wait_ge(normed, N_X1ROWS)
                dve.wait_ge(tile_ready, U_GB + j + 1)
                v.tensor_tensor(z[:], psum(U_GB + j), rstd[:], ALU.mult
                                ).then_inc(tile_read, 1)

            def mix_g(j):
                dve.wait_ge(g_gelu, j + 1)
                out = halves(rows[:, HA + HM + j, :])
                v.tensor_tensor(out, z[:], out, ALU.mult).then_inc(mixed, 1)
                dve.wait_ge(mixed, j + 1)

            for beat in range(12):
                if beat % 4 == 0:
                    lo(U_GB + 1 + beat // 4)
                if beat == 0:
                    read_v(U_GB - 1, HM + HA - 1)
                head(HM + HA - 1, beat)
                if beat in (6, 10):
                    read_g(beat // 4 - 1)
                if beat in (7, 11):
                    mix_g(beat // 4 - 1)
            lo(U_OUT)
            for j in (2, 3):
                read_g(j)
                mix_g(j)
            split_rows(2 * KT, None, ROWS, lambda: lo(U_OUT + 1))

            def add_mix(m, mm, more=0):
                t = U_OUT + m
                dve.wait_ge(tile_ready, t + 1 + more)
                if isinstance(mm, int):
                    x = halves(rows[:, mm, :])
                else:
                    x = rows[:, bass.ds(mm, 1), :].rearrange("p o (c n) -> p (o c) n", c=2)
                v.tensor_tensor(x, psum(t), x, ALU.add).then_inc(tile_read, 1)

            for n in range(4):
                dve.wait_ge(x_again[n], 16)
            for m in range(3):
                lo(U_OUT + m + 2)
                add_mix(m, m)
            with dve.Fori(0, 3) as i:
                for n in range(4):
                    lo(U_OUT + 5 + n, 4 * i)
                    add_mix(3 + n, 4 * i + 3 + n, 4 * i)
            add_mix(KT - 1, KT - 1)
            dve.wait_ge(tile_read, U_FF)
            split_rows(3 * KT, "g_ffn", ROWS, lambda: lo(U_FF + 1))
            row_factor(N_X1ROWS, sd1)
            dve.wait_ge(edges, 2)

            def up_tile(g, i, gr, t, unit, held):
                kind, j, gate = unit
                if kind == "down":
                    return
                e = 2 * GROUP * g + 2 * j + gate
                buf, out = upb[gate], cv[gate]
                src = slots[t % 4]
                dve.wait_ge(tile_ready, t + 1 + FF_TILES * i)
                body = buf[:, CF - 1:CF - 1 + ROWS].rearrange("p (c n) -> p c n", c=2)[:, :, 0:BODY]
                tail = buf[:, 0:up_w].rearrange("p (c n) -> p c n", c=2)[:, :, CF - 1 + BODY:]
                v.tensor_tensor(body, src[:, :, 0:BODY], rstd[:, :, 0:BODY], ALU.mult)
                v.tensor_tensor(tail, src[:, :, BODY:HALF], rstd[:, :, BODY:HALF], ALU.mult
                                ).then_inc(tile_read, 1)
                dve.wait_ge(tile_read, t + 1 + FF_TILES * i)
                tile = gate * FT + GROUP * gr + j
                n = 2 * tile + PAR["past_f"]
                past_f = par[:, n:n + 2] if isinstance(tile, int) else par[:, bass.ds(n, 2)]
                v.tensor_copy(buf[:, CF - 1 + SEQ:2 * (CF - 1) + SEQ], past_f)
                kept = f_last[:, tile, :] if isinstance(tile, int) else \
                    f_last[:, bass.ds(tile, 1), :].rearrange("p o n -> p (o n)")
                lasts = buf[:, SEQ:].rearrange("p (c n) -> p c n", c=2)[:, :, 0:CF - 1]
                v.tensor_copy(kept.rearrange("p (c n) -> p c n", c=2), lasts).then_inc(up_ready, 1)
                dve.wait_ge(f_tap, e + 1 + 2 * GROUP * i)
                dve.wait_ge(up_ready, e + 1 + 2 * GROUP * i)
                link(v.scalar_tensor_tensor(out[:], buf[:, 1:up_w - 1], col("conv_f_w", tile + 2 * FT),
                                            out[:], ALU.mult, ALU.add))
                last = v.scalar_tensor_tensor(out[:], buf[:, 0:up_w - 2], col("conv_f_w", tile),
                                              out[:], ALU.mult, ALU.add)
                if not gate:
                    link(last)
                    return
                last.then_inc(gate_conv, 1)
                dve.wait_ge(gate_gelu, GROUP * g + j + 1 + GROUP * i)
                v.tensor_tensor(cv[0][:], cv[1][:], cv[0][:], ALU.mult).then_inc(h_ready, 1)
                if not held:
                    low_h(g, i, j)

            def low_h(g, i, j):
                dve.wait_ge(h_hi, GROUP * g + j + 1 + GROUP * i)
                v.tensor_tensor(hl[:, j, 0:SEQ], cv[0][:, 0:SEQ], hh[:, j, 0:SEQ].bitcast(F32), ALU.subtract)
                v.tensor_tensor(hl[:, j, SEQ:ROWS], cv[0][:, SEQ + CF - 1:],
                                hh[:, j, SEQ:ROWS].bitcast(F32), ALU.subtract).then_inc(h_lo, 1)

            def add_down(u, q, more=0):
                t = tiles_through(u) - DOWN_TILES
                for n in range(DOWN_TILES):
                    x = halves(rows[:, DOWN_TILES * q + n, :])
                    dve.wait_ge(tile_ready, t + n + 1 + more)
                    v.tensor_tensor(x, slots[(t + n) % 4][:, :, 0:HALF], x, ALU.add).then_inc(tile_read, 1)

            def feed(g0, i=0, gr=0):
                order = ff_order(g0)
                u = U_FF if g0 == 0 else U_LOOP
                for pos, (kind, q, _) in enumerate(order):
                    if not (g0 == 0 and pos == 0):
                        lo(u + pos + 1, FF_PER * i)
                    if pos or g0:
                        last = order[pos - 1] if pos else ("up", GROUP - 1, 1)
                        t = tiles_through(u + pos - 1) - 1
                        gg, rr = (g0, gr) if pos else (g0 - 1, gr - 1)
                        up_tile(gg, i, rr, t, last, pos == 2 and g0)
                    if kind == "down":
                        add_down(u + pos, q, FF_TILES * i)
                    if g0 and pos == 2 + DOWN:
                        low_h(g0, i, 0)

            feed(0)
            with dve.Fori(0, NG - 1) as i:
                chain.enter(i, 3 * GROUP)
                feed(1, i, i + 1)
                chain.leave(NG - 1)
            lo(U_LAST + 1)
            up_tile(NG - 1, 0, NG - 1, tiles_through(U_LAST - 1) - 1, ("up", GROUP - 1, 1), False)
            for q in range(DOWN):
                if 0 < q < DOWN - 1:
                    lo(U_LAST + q + 1)
                add_down(U_LAST + q, q)

        @block.tensor
        def _(pe):
            mm = nc.tensor.matmul

            def products(out, weights, high, low, first, last):
                w_high, w_low = weights
                for c, (dst, hs, ls) in enumerate(zip(out, high, low)):
                    mm(dst, w_high, hs, start=first, stop=False)
                    mm(dst, w_high, ls, start=False, stop=False)
                for c, (dst, hs) in enumerate(zip(out, high)):
                    ins = mm(dst, w_low, hs, start=False, stop=last)
                return ins

            def unit(u, between=lambda beat: None, more=0, first=None, width=ROWS, tiles=None, bank=None):
                pe.wait_ge(lo_split, u + 1 + more)
                t = tiles_through(u) - 1
                tiles = more if tiles is None else tiles
                slot = slots[t % 2] if bank is None else slots[bank]
                reuse = 2 if bank is None or t < U_FF + 2 else 4
                if t >= reuse:
                    pe.wait_ge(tile_read, t - reuse + 1 + tiles)
                n = [(0, width)] if width < HALF else [(0, HALF), (HALF, ROWS)]
                out = [slot[:, c, 0:b - a] for c, (a, b) in enumerate(n)]
                w = [buf[:, u % 2, :].rearrange("p (k n) -> p k n", k=KT) for buf in (wh, wl)]
                for k in range(KT):
                    if first is not None:
                        pe.wait_ge(xlo, first + k + 1)
                    ins = products(out, [x[:, k, :] for x in w], [xh[:, k, a:b] for a, b in n],
                                   [xl[:, k, a:b] for a, b in n], k == 0, k == KT - 1)
                    if k == KT - 1:
                        ins.then_inc(tile_ready, 1)
                    if k % 4 == 3:
                        between(k // 4)

            def mean(n, matrix, square, more=0, width=ROWS):
                if n > 0:
                    pe.wait_ge(roots_ready, n + more)
                if width < ROWS:
                    mm(means[:, 0, 0:width], matrix[:], square[:, 0:width],
                       start=True, stop=True).then_inc(means_ready, 1)
                    return
                for c in range(2):
                    ins = mm(means[:, c, 0:HALF], matrix[:], square[:, c * HALF:(c + 1) * HALF],
                             start=True, stop=True)
                ins.then_inc(means_ready, 1)

            def flat(ap):
                return ap.rearrange("p c n -> p (c n)")

            def head_mean(n, count, more=0, width=ROWS):
                pe.wait_ge(squares, count + more)
                mean(n, mean_head, flat(sq[:]), more, width)

            def score(a, t, more=0):
                if a or t:
                    pe.wait_ge(logits_ready, TILES * a + t + TILES * more)
                s = a % 2
                if t == 0:
                    n = N_QM + a + 1 if a < HM else N_HEAD + 2 * (a - HM) + 2
                    pe.wait_ge(normed, n + 2 * more)
                if t == Q_TILES:
                    pe.wait_ge(past_in[s], 32 * (a // 2 + 1) + 16 * more)
                q = q_m[s] if a < HM else qT[:, :]
                cached = flat(past[:, s, 0:2, :])
                if t < Q_TILES:
                    key = memk[:, a, :] if a < HM else kT[:, 0:keys(a, t)]
                    ins = mm(scores[:, 0:keys(a, t)], q[:, t * P:(t + 1) * P], key, start=True, stop=True)
                elif a < HM:
                    ins = mm(scores[0:DEC, 0:N_MEM], q[:, SEQ:ROWS], cached, start=True, stop=True)
                else:
                    mm(scores[0:DEC, 0:PAST], q[:, SEQ:ROWS], cached[:, 0:PAST], start=True, stop=True)
                    ins = mm(scores[0:DEC, PAST:PAST + DEC], q[:, SEQ:ROWS], kT[:, SEQ:ROWS],
                             start=True, stop=True)
                ins.then_inc(scores_ready, 1)

            def flip_free(w, more=0):
                if w:
                    pe.wait_ge(flip_read, w + more)

            def turn(dst, src):
                n = src.shape[0]
                return nc.tensor.transpose(dst, src, ident[0:n, 0:n])

            def flip_prob(a, t, more=0):
                w = flips_before(a) + (2 if a >= HM else 0) + t
                pe.wait_ge(probs_ready, TILES * a + t + 1 + TILES * more)
                flip_free(w, PER_A * more)
                if t < Q_TILES:
                    for c in range(keys(a, t) // P):
                        ins = turn(flip[:, c * P:(c + 1) * P], prob[t][:, c * P:(c + 1) * P])
                else:
                    apart(pe, more)
                    turn(flip[:, 0:DEC], prob[t][0:DEC, 0:P])
                    n = P if a < HM else DEC
                    ins = turn(flip[0:n, DEC:2 * DEC], prob[t][0:DEC, P:P + n])
                ins.then_inc(flip_ready, 1)

            def flip_memory(m):
                pe.wait_ge(tile_read, HM + m + 1)
                flip_free(m)
                for c in range(2):
                    ins = turn(flip[:, c * P:(c + 1) * P], vT[:, c * P:(c + 1) * P])
                ins.then_inc(flip_ready, 1)

            def flip_v(h, s, more=0):
                pe.wait_ge(tile_read, U_HEAD + PER_H * (h + 1) + PER_H * more)
                flip_free(flips_before(HM + h) + s, PER_A * more)
                if s == 0:
                    for t in range(Q_TILES):
                        ins = turn(flip[:, t * P:(t + 1) * P], vT[:, t * P:(t + 1) * P])
                else:
                    ins = turn(flip[0:DEC, 0:P], vT[:, SEQ:ROWS])
                ins.then_inc(flip_ready, 1)

            def output(a, s, more=0):
                flip_free(flips_before(a + 1) - 2 + s, PER_A * more)
                if s == 0:
                    for t in range(Q_TILES):
                        n = keys(a, t) // P
                        for c in range(n):
                            value = memv[:, a, c, :] if a < HM else v_rows[:, c, :]
                            at = probT_at(a, t) + c * P
                            ins = mm(flip[:, t * P:(t + 1) * P], value, probT[:, at:at + P],
                                     start=c == 0, stop=c == n - 1)
                else:
                    at = probT_at(a, Q_TILES)
                    mm(flip[:, 0:DEC], past[:, a % 2, 2, :], probT[:, at:at + DEC], start=True, stop=False)
                    if a < HM:
                        ins = mm(flip[:, 0:DEC], past[:, a % 2, 3, :], probT[:, at + DEC:at + 2 * DEC],
                                 start=False, stop=True)
                    else:
                        ins = mm(flip[:, 0:DEC], v_rows[0:DEC, Q_TILES, :],
                                 probT[0:DEC, at + DEC:at + 2 * DEC], start=False, stop=True)
                ins.then_inc(flip_ready, 1)

            def memory_head(m, beat):
                if beat < TILES:
                    score(m, beat)
                if 2 <= beat < 2 + TILES:
                    flip_prob(m, beat - 2)
                if beat == 7:
                    output(m, 0)

            def band_head(h, beat, i=0):
                a, more = HM + h, 2 * i
                if beat < TILES:
                    score(a, beat, more)
                if beat in (1, 2):
                    flip_v(h, beat - 1, more)
                if 3 <= beat < 3 + TILES:
                    flip_prob(a, beat - 3, more)
                if beat in (8, 9):
                    output(a, beat - 8, more)

            def gate(j, n):
                pe.wait_ge(conv_ready, j + 1)
                pe.wait_ge(roots_ready, N_QM + j + 1)
                if j or n:
                    pe.wait_ge(gate_exp, 2 * j + n)
                for c in range(2):
                    ins = mm(means[:, c, 0:HALF], rg[:, n, j, :], xc[:, c * HALF:(c + 1) * HALF],
                             start=True, stop=True)
                ins.then_inc(gate_ready, 1)

            pe.wait_ge(consts, 6)

            def mem_between(u):
                def between(beat):
                    if beat < 3:
                        return
                    if u == 0:
                        pe.wait_ge(sums_ready, 1)
                        mean(N_MEMROWS, mean_rows, sum0, width=N_MEM)
                    elif u <= HM:
                        head_mean(N_MEMK + u - 1, u, width=N_MEM)
                    else:
                        flip_memory(u - HM - 1)
                return between

            for u in range(U_QX):
                unit(u, mem_between(u), width=N_MEM, first=0 if u == 0 else None)

            def x_between(beat):
                if beat == 1:
                    flip_memory(HM - 1)
                if beat == 3:
                    pe.wait_ge(sums_ready, 2)
                    mean(N_XROWS, mean_rows, sum0)

            pe.wait_ge(gates_in, 16 * 4)
            for m in range(HM):
                u = U_QX + 2 * m

                def q_between(beat, m=m):
                    if m == 0:
                        x_between(beat)
                        return
                    if beat == 0 and m >= 2:
                        output(m - 2, 1)
                    memory_head(m - 1, beat)
                    if beat in (2, 3):
                        gate(m - 1, beat - 2)

                def x_b_between(beat, m=m):
                    if beat == 1:
                        if m:
                            pe.wait_ge(gate_exp, 2 * m)
                        head_mean(N_QM + m, HM + m + 1)
                    if m:
                        memory_head(m - 1, 4 + beat)

                unit(u, q_between, first=KT if m == 0 else None)
                unit(u + 1, x_b_between)

            def head_unit(h, n, i=0):
                def between(beat):
                    b = 4 * n + beat
                    if h == 0:
                        if b == 0:
                            output(HM - 2, 1)
                        if b < 8:
                            memory_head(HM - 1, b)
                        if b == 8:
                            output(HM - 1, 1)
                        if b in (2, 3):
                            gate(HM - 1, b - 2)
                    if b in (5, 9):
                        if h == 0:
                            pe.wait_ge(gate_exp, 2 * RT)
                        qk = b // 4 - 1
                        head_mean(N_HEAD + 2 * h + qk, 2 * HM + 2 * h + qk + 1, 4 * i)
                    if h >= 1:
                        band_head(h - 1, b, i)

                unit(U_HEAD + PER_H * h + n, between, 2 * PER_H * i)

            for h in range(2):
                for n in range(PER_H):
                    head_unit(h, n)
            with pe.Fori(0, 3) as i:
                for h in (2, 3):
                    for n in range(PER_H):
                        head_unit(h, n, i)
            for j in range(RT):
                unit(U_GB + j, lambda beat, j=j: band_head(HA - 1, 4 * j + beat))
            for m in range(4):
                unit(U_OUT + m, first=2 * KT if m == 0 else None)
            with pe.Fori(0, 3) as i:
                for m in range(4):
                    unit(U_OUT + 4 + m, more=4 * i)

            pe.wait_ge(flip_read, flips_before(HM + HA))

            def down(u, i=0, g=0):
                pe.wait_ge(lo_split, u + 1 + FF_PER * i)
                t0 = tiles_through(u) - DOWN_TILES
                w = [buf[:, u % 2, :].rearrange("p (k n) -> p k n", k=GROUP) for buf in (wh, wl)]
                for n in range(DOWN_TILES):
                    t = t0 + n
                    pe.wait_ge(tile_read, t - 3 + FF_TILES * i)
                    out = [slots[t % 4][:, c, 0:HALF] for c in range(2)]
                    for k in range(GROUP):
                        parts = [[x[:, k, c * HALF:(c + 1) * HALF] for c in range(2)] for x in (hh, hl)]
                        ins = products(out, [x[:, k, n * P:(n + 1) * P] for x in w], *parts,
                                       k == 0, k == GROUP - 1)
                    ins.then_inc(tile_ready, 1)

            def feed(g0, i=0):
                u = U_FF if g0 == 0 else U_LOOP
                for pos, (kind, j, _) in enumerate(ff_order(g0)):
                    if kind == "down":
                        if j == 0:
                            pe.wait_ge(h_lo, GROUP * g0 + GROUP * i)
                        down(u + pos, i)
                        continue
                    t = tiles_through(u + pos) - 1
                    if t == U_FF + 3:
                        pe.wait_ge(roots_ready, N_X1ROWS + 1)

                    def between(beat, t=t):
                        if t == U_FF and beat == 3:
                            pe.wait_ge(sums_ready, 3)
                            mean(N_X1ROWS, mean_rows, sum1)

                    unit(u + pos, between, FF_PER * i, first=3 * KT if t == U_FF else None,
                         tiles=FF_TILES * i, bank=t % 4)

            feed(0)
            with pe.Fori(0, NG - 1) as i:
                feed(1, i)
            pe.wait_ge(h_lo, GROUP * NG)
            for q in range(DOWN):
                down(U_LAST + q)


_INS = ["xT", "memT", "cache_kT", "cache_v", "cache_mkT", "cache_mv", "params", "rel_table",
        "w_in", "w_mem_kv", "w_rg_a", "w_rg_i", "w_out", "w_up", "w_down"]
_OUTS = [("yT", (D, ROWS)), ("kT", (HA, P, ROWS)), ("vT", (HA, P, ROWS)), ("mkT", (HM, P, N_MEM)),
         ("mvT", (HM, P, N_MEM)), ("b_conv", (P, RT, 2 * (CB - 1))), ("b_h", (P, RT, 2)),
         ("f_conv", (P, 2 * FT, 4))]


def kernel(**inputs):
    import numpy as np
    import concourse.bacc as bacc
    from concourse import mybir as mb
    from concourse.bass_utils import run_bass_kernel_spmd

    a = {name: np.asarray(x) for name, x in inputs.items()}

    def tiles(x):
        x = x.reshape(*x.shape[:-1], x.shape[-1] // P, P)
        return np.moveaxis(x, -1, 0).reshape(P, -1)

    def past(x):
        x = x.reshape(x.shape[0], -1, P)
        return x.transpose(2, 1, 0).reshape(P, -1)

    parts = [tiles(a["g_attn"][0]), tiles(a["g_mem"][0]), tiles(a["g_ffn"][0]),
             tiles(a["g_q_a"][0]), tiles(a["g_k_a"][0]), tiles(a["g_q_m"][0]), tiles(a["g_k_m"][0]),
             tiles(a["conv_b_w"][0]), tiles(a["conv_b_b"][0]), tiles(a["b_rg_a"][0]),
             tiles(a["b_rg_i"][0]), tiles(a["lru_lambda"][0]), tiles(a["state_b_h"][0, 0]),
             past(a["cache_b_conv"][0, 0]), tiles(a["conv_f_w"][0]), tiles(a["conv_f_b"][0]),
             past(a["cache_f_conv"][0, 0])]
    laid = {
        "xT": np.concatenate([a["x_prompt"][0], a["x_sample"][0]]).T,
        "memT": a["mem_prompt"][0].T,
        "cache_kT": a["cache_a_k"][0, 0].transpose(1, 2, 0),
        "cache_v": a["cache_a_v"][0, 0],
        "cache_mkT": a["cache_mem_k"][0, 0].transpose(1, 2, 0),
        "cache_mv": a["cache_mem_v"][0, 0],
        "params": np.concatenate(parts, axis=1),
        "rel_table": a["rel_table"][0],
        **{name: a[name][0] for name in _INS[8:]},
    }
    nc = bacc.Bacc("TRN2", target_bir_lowering=False, num_devices=1)
    arrays, args = {}, []
    for name in _INS:
        x = np.ascontiguousarray(laid[name])
        arrays[f"in_{name}"] = x
        args.append(nc.dram_tensor(f"in_{name}", x.shape, mb.dt.from_np(x.dtype),
                                   kind="ExternalInput").ap())
    for name, shape in _OUTS:
        args.append(nc.dram_tensor(f"out_{name}", shape, mb.dt.from_np(np.dtype(np.float32)),
                                   kind="ExternalOutput").ap())
    encoder(nc, *args)
    r = run_bass_kernel_spmd(nc, [arrays], core_ids=[0]).results[0]
    y, k, v, mk, mv, bc, bh, fc = (r[f"out_{name}"] for name, _ in _OUTS)
    y = y.T
    k, v = k.transpose(2, 0, 1), v.transpose(2, 0, 1)
    mk, mv = mk.transpose(2, 0, 1), mv.transpose(2, 0, 1)

    def rows_of(x, n):
        return np.ascontiguousarray(x.transpose(2, 1, 0).reshape(n, -1))[None, None]

    return tuple(np.ascontiguousarray(x) for x in (
        y[None, :SEQ], y[None, SEQ:],
        k[None, None, :SEQ], v[None, None, :SEQ], mk[None, None], mv[None, None],
        rows_of(bc[:, :, :CB - 1], CB - 1), rows_of(bh[:, :, :1], 1)[:, :, 0],
        rows_of(fc[:, :, :CF - 1], CF - 1),
        k[None, None, SEQ:], v[None, None, SEQ:],
        rows_of(bc[:, :, CB - 1:], CB - 1), rows_of(bh[:, :, 1:], 1)[:, :, 0],
        rows_of(fc[:, :, CF - 1:], CF - 1)))
```

```python
from contextlib import ExitStack

import concourse.bass as bass
from concourse import mybir

ALU = mybir.AluOpType
ACT = mybir.ActivationFunctionType
F32 = mybir.dt.float32
F32R = mybir.dt.float32r

P = 128
D = 2048
KT = D // P
SEQ, DEC = 512, 32
ROWS = SEQ + DEC
HALF = ROWS // 2
BODY = SEQ - HALF
N_MEM = 256
HA, HM = 8, 4
D_A, D_M, D_RNN = HA * P, HM * P, 512
RT = D_RNN // P
PAST = 128
D_FF = 6144
FT = D_FF // P
CB, CF = 4, 3
GROUP = 4
NG = FT // GROUP
EPS = 1e-6
MASKED = -1e30
CHUNK = 64
REL = 256
Q_TILES = SEQ // P
TILES = Q_TILES + 1
EXT = 640
PER_H = 3

U_MEM = 0
U_QX = U_MEM + 2 * HM
U_HEAD = U_QX + 2 * HM
U_GB = U_HEAD + 3 * HA
U_OUT = U_GB + RT
U_FF = U_OUT + KT
UP, DOWN = 2 * GROUP, KT * GROUP // 16
FF_PER = UP + DOWN
U_LOOP = U_FF + UP
DOWN_TILES = 16 // GROUP
FF_TILES = UP + KT
U_LAST = U_LOOP + FF_PER * (NG - 1)

PAR = {}
_n = 0
for _name, _w in (("g_attn", KT), ("g_mem", KT), ("g_ffn", KT), ("g_q_a", 1), ("g_k_a", 1),
                  ("g_q_m", 1), ("g_k_m", 1), ("conv_b_w", CB * RT), ("conv_b_b", RT),
                  ("b_rg_a", RT), ("b_rg_i", RT), ("lam", RT), ("h0", RT),
                  ("past_b", (CB - 1) * RT), ("conv_f_w", CF * 2 * FT), ("conv_f_b", 2 * FT),
                  ("past_f", (CF - 1) * 2 * FT)):
    PAR[_name] = _n
    _n += _w
N_PAR = _n

N_MEMROWS = 0
N_MEMK = 1
N_XROWS = N_MEMK + HM
N_QM = N_XROWS + 1
N_HEAD = N_QM + HM
N_X1ROWS = N_HEAD + 2 * HA

W_MEMV = 0
W_M = W_MEMV + HM
PER_M = TILES + 2
W_A = W_M + PER_M * HM
PER_A = 2 + TILES + 2


def tiles_through(u):
    if u < U_LOOP:
        return u + 1
    full, pos = divmod(u - U_LOOP, FF_PER)
    if full == NG - 1:
        own = DOWN_TILES * (pos + 1)
    elif pos < 2:
        own = pos + 1
    elif pos < 2 + DOWN:
        own = 2 + DOWN_TILES * (pos - 1)
    else:
        own = KT + pos - DOWN + 1
    return U_LOOP + FF_TILES * full + own


def encoder(nc, xT, memT, cache_kT, cache_v, cache_mkT, cache_mv, params, rel_table, w_in,
            w_mem_kv, w_rg_a, w_rg_i, w_out, w_up, w_down,
            yT, kT_out, vT_out, mkT_out, mvT_out, b_conv_out, b_h_out, f_conv_out):
    with ExitStack() as ctx:
        def sb(name, shape, dt=F32):
            return ctx.enter_context(nc.sbuf_tensor(name, shape, dt))

        def sem(name):
            return ctx.enter_context(nc.semaphore(name))

        up_w = ROWS + 2 * (CF - 1)
        UP_W = up_w + DEC

        rows = sb("rows", [P, KT, ROWS])
        xh = sb("xh", [P, KT, ROWS], F32R)
        xl = sb("xl", [P, KT, ROWS], F32R)
        raw = sb("raw", [P, 2, 16 * P])
        wh = sb("wh", [P, 2, 16 * P], F32R)
        wl = sb("wl", [P, 2, 16 * P], F32R)
        par = sb("par", [P, N_PAR])
        rstd = sb("rstd", [P, 2, HALF])
        eps = sb("eps", [P, 1])
        zero = sb("zero", [P, 1])
        mean_rows = sb("mean_rows", [P, P])
        f_last = sb("f_last", [P, 2 * FT, 4])
        overlay = nc.sbuf_base

        def place(cursor, name, shape, dt=F32):
            size = 4
            for n in shape[1:]:
                size *= n
            t = nc.alloc_sbuf_tensor_at(name, shape, dt, offset=overlay + cursor[0])
            cursor[0] += -(-size // 32) * 32
            return t

        at = [0]
        ident = place(at, "ident", [P, P])
        mean_head = place(at, "mean_head", [P, P], F32R)
        z = place(at, "z", [P, 2, HALF])
        behind_z = list(at)
        sq_high = place(at, "sq_high", [P, 2, HALF], F32R)
        sq_low = place(at, "sq_low", [P, 2, HALF], F32R)
        sq, sd = place(behind_z, "sq", [P, 2, HALF]), place(behind_z, "sd", [P, 2, HALF])
        vT = place(at, "vT", [P, ROWS])
        memk = place(at, "memk", [P, HM, N_MEM])
        memv = place(at, "memv", [P, HM, 2, P])
        qT = place(at, "qT", [P, ROWS])
        kT = place(at, "kT", [P, ROWS])
        v_rows = place(at, "v_rows", [P, TILES, P])
        prob = [place(at, f"prob{t}", [P, max(t + 1, 2) * P]) for t in range(Q_TILES)]
        prob.append(place(at, "prob_s", [P, N_MEM]))
        probT = place(at, "probT", [P, 10 * P + 2 * DEC])
        bias = place(at, "bias", [P, 2, SEQ])
        past = place(at, "past", [P, 2, 4, P])
        rg = place(at, "rg", [P, 2, RT, P])
        xb = place(at, "xb", [P, ROWS + 2 * (CB - 1)])
        scale_q = place(at, "scale_q", [P, 2])
        lam = place(at, "lam", [P, 7, RT])
        row_max = place(at, "row_max", [P, TILES])
        row_neg = place(at, "row_neg", [P, TILES])
        row_sum = place(at, "row_sum", [P, TILES])
        row_inv = place(at, "row_inv", [P, TILES])
        b_last = place(at, "b_last", [P, RT, 2 * (CB - 1)])
        h_last = place(at, "h_last", [P, RT, 2])
        assert overlay + at[0] <= nc.sbuf_top, (at, nc.sbuf_top - overlay)
        at_ff = [0]
        hh = place(at_ff, "hh", [P, GROUP, ROWS], F32R)
        hl = place(at_ff, "hl", [P, GROUP, ROWS], F32R)
        upb = [place(at_ff, f"up{n}", [P, UP_W]) for n in range(2)]
        cv = [place(at_ff, f"conv{n}", [P, ROWS + CF - 1]) for n in range(2)]
        sd1 = place(at_ff, "sd1", [P, 2, HALF])
        sum1 = place(at_ff, "sum1", [P, ROWS])
        sq1 = place(at_ff, "sq1", [P, ROWS])
        assert overlay + at_ff[0] <= nc.sbuf_top, (at_ff, nc.sbuf_top - overlay)
        xc, ga, gi, dec, tan = (rows[:, n, :] for n in range(5))
        q_m = [rows[:, 5, :], rows[:, 6, :]]
        sum0, sq0 = qT[:, :], kT[:, :]
        mem_squares = [t[:, c, 0:N_MEM] for t in (z, sq, sd) for c in range(2)]
        mem_squares += [vT[:, 0:N_MEM], vT[:, N_MEM:2 * N_MEM]]
        x_squares = [bias[:].rearrange("p c n -> p (c n)"), past[:].rearrange("p a c n -> p (a c n)"),
                   v_rows[:].rearrange("p t n -> p (t n)"), xb[:, CB - 1:]]
        x_squares = [t[:, 0:ROWS] for t in x_squares]
        spread, table = probT[0:HA, 0:EXT], probT[0:HA, EXT:EXT + 2 * REL + 1]

        slots = [ctx.enter_context(nc.psum_tensor(f"out{n}", [P, 2, 512], F32)) for n in range(4)]
        scores, flip = slots[2][:, 0, :], slots[2][:, 1, :]
        means = slots[3]

        ext_dram = nc.dram_tensor("bias_by_distance", [HA, EXT], F32, kind="Internal")
        skew_dram = nc.dram_tensor("bias_skewed", [HA, P, SEQ], F32, kind="Internal")

        raw_loaded = [sem("raw_loaded0"), sem("raw_loaded1")]
        hi_split = sem("hi_split")
        lo_split = sem("lo_split")
        tile_ready = sem("tile_ready")
        tile_read = sem("tile_read")
        xhi = sem("xhi")
        xlo = sem("xlo")
        rows_used = sem("rows_used")
        params_in = sem("params_in")
        conv_f_in = sem("conv_f_in")
        mem_in = [sem(f"mem_in{n}") for n in range(4)]
        x_in = [sem(f"x_in{n}") for n in range(4)]
        x_again = [sem(f"x_again{n}") for n in range(4)]
        table_in = sem("table_in")
        spread_ready = sem("spread_ready")
        ext_stored = sem("ext_stored")
        skew_stored = sem("skew_stored")
        bias_in = [sem("bias_in0"), sem("bias_in1")]
        bias_masked = sem("bias_masked")
        past_in = [sem("past_in0"), sem("past_in1")]
        rg_zeroed = sem("rg_zeroed")
        gates_in = sem("gates_in")
        consts = sem("consts")
        set_apart = sem("set_apart")
        pool_step = sem("pool_step")
        dve_step = sem("dve_step")
        act_step = sem("act_step")
        row_squares = sem("row_squares")
        sums_ready = sem("sums_ready")
        prepared = sem("prepared")
        lam_ready = sem("lam_ready")
        lam_exp = sem("lam_exp")
        squares = sem("squares")
        squares_low = sem("squares_low")
        means_ready = sem("means_ready")
        roots_ready = sem("roots_ready")
        normed = sem("normed")
        scores_ready = sem("scores_ready")
        logits_ready = sem("logits_ready")
        exps_ready = sem("exps_ready")
        probs_ready = sem("probs_ready")
        flip_ready = sem("flip_ready")
        flip_read = sem("flip_read")
        k_out = sem("k_out")
        v_out = sem("v_out")
        mk_out = sem("mk_out")
        mv_out = [sem("mv_out0"), sem("mv_out1")]
        xb_ready = sem("xb_ready")
        b_tap = sem("b_tap")
        conv_ready = sem("conv_ready")
        gate_ready = sem("gate_ready")
        gate_open = sem("gate_open")
        decay_ready = sem("decay_ready")
        ratio_ready = sem("ratio_ready")
        scale_ready = sem("scale_ready")
        g_gelu = sem("g_gelu")
        mixed = sem("mixed")
        edges = sem("edges")
        up_ready = sem("up_ready")
        f_tap = sem("f_tap")
        gate_conv = sem("gate_conv")
        gate_gelu = sem("gate_gelu")
        h_ready = sem("h_ready")
        h_hi = sem("h_hi")
        h_lo = sem("h_lo")
        y_out = sem("y_out")
        small_out = sem("small_out")

        def col(name, n=0):
            if isinstance(n, int):
                return par[:, PAR[name] + n:PAR[name] + n + 1]
            return par[:, bass.ds(n + PAR[name], 1)]

        def halves(ap):
            return ap.rearrange("p (c n) -> p c n", c=2)

        def k_major(w):
            return w.rearrange("(k p) n -> p k n", p=P)

        def flips_before(a):
            return W_M + PER_M * a if a <= HM else W_A + PER_A * (a - HM)

        def keys(a, t):
            if a < HM:
                return N_MEM
            return (t + 1) * P if t < Q_TILES else PAST + DEC

        def probT_at(a, t):
            if a < HM:
                return t * N_MEM
            return t * (t + 1) // 2 * P

        def mem_bank(t):
            return slots[t % 2][:, t // 2 % 2, 0:N_MEM]

        def mem_vT(n):
            return vT[:, n % 2 * N_MEM:(n % 2 + 1) * N_MEM]

        def mem_steps(u):
            return {3: [("k", 0)], 4: [("k", 1)], 5: [("k", 2)], 6: [("k", 3), ("v", 0)],
                    7: [("v", 1), ("v", 2)]}.get(u, [])

        def x_early(u):
            return {6: range(0, 6), 7: range(6, KT)}.get(u, range(0))

        def ff_order(g):
            order = []
            for j in range(GROUP):
                order += [("up", j, 0), ("up", j, 1)]
                if j == 0 and g > 0:
                    order += [("down", q, 0) for q in range(DOWN)]
            return order

        def apart(engine, more):
            if not isinstance(more, int):
                engine.sem_inc(set_apart, 1)

        class Chain:

            def __init__(self, engine, semaphore):
                self.engine, self.semaphore, self.n, self.more = engine, semaphore, 0, 0

            def link(self, instruction):
                self.n += 1
                instruction.then_inc(self.semaphore, 1)
                self.engine.wait_ge(self.semaphore, self.n + self.more)

            def enter(self, i, per):
                self.at, self.per, self.more = self.n, per, per * i

            def leave(self, rounds):
                assert self.n - self.at == self.per, (self.n - self.at, self.per)
                self.n, self.more = self.n + self.per * (rounds - 1), 0

        block = ctx.enter_context(nc.Block())

        @block.sync
        def _(sp):
            def load(u, src, more=0):
                if u >= 2:
                    sp.wait_ge(hi_split, u - 1 + more)
                    sp.wait_ge(lo_split, u - 1 + more)
                    apart(sp, more)
                sp.dma_start(raw[:, u % 2, :].rearrange("p (k n) -> p k n", k=src.shape[1]),
                             src).then_inc(raw_loaded[u % 2], 16)

            def mem_w(c):
                return k_major(w_mem_kv)[:, :, c * P:(c + 1) * P]

            def in_w(c):
                return k_major(w_in)[:, :, bass.ds(c, P)]

            def load_past(a, keys, values):
                n = keys.shape[1] // P
                sp.dma_start(past[:, a % 2, 0:n, :].rearrange("p c n -> p (c n)"),
                             keys).then_inc(past_in[a % 2], 16)
                sp.dma_start(past[:, a % 2, 2:2 + n, :], values).then_inc(past_in[a % 2], 16)

            def m_past(m):
                if m == 0:
                    sp.wait_ge(sums_ready, 2)
                if m >= 2:
                    sp.wait_ge(flip_ready, flips_before(m - 1))
                load_past(m, cache_mkT[m],
                          cache_mv.rearrange("(c p) h d -> h p c d", p=P)[m])

            def head_loads(h, hr, flips=0, logits=0):
                sp.wait_ge(flip_ready, flips_before(HM + h - 1) + flips)
                if h >= 1:
                    apart(sp, logits)
                    sp.wait_ge(logits_ready, TILES * (HM + h - 1) + logits)
                apart(sp, logits)
                sp.dma_start(bias[:, h % 2, :], skew_dram.ap()[hr] if isinstance(hr, int) else
                             skew_dram.ap()[bass.ds(hr, 1)].rearrange("o p n -> (o p) n")
                             ).then_inc(bias_in[h % 2], 16)
                if isinstance(hr, int):
                    keys, values = cache_kT[hr], cache_v[:, hr, :]
                else:
                    keys = cache_kT[bass.ds(hr, 1)].rearrange("o p n -> (o p) n")
                    values = cache_v[:, bass.ds(hr, 1), :]
                    values = values.rearrange("p o n -> p (o n)")
                load_past(h, keys, values.rearrange("p (c n) -> p c n", c=1))

            def store(dst, h, src, semaphore):
                out = dst[h] if isinstance(h, int) else dst[bass.ds(h, 1)].rearrange("o p n -> (o p) n")
                sp.dma_start(out, src).then_inc(semaphore, 16)

            def store_k(h, hr, more=0):
                sp.wait_ge(normed, N_HEAD + 2 * h + 2 + 2 * more)
                apart(sp, more)
                store(kT_out, hr, kT[:, :], k_out)

            def store_v(h, hr, more=0):
                sp.wait_ge(tile_read, U_HEAD + PER_H * (h + 1) + PER_H * more)
                apart(sp, more)
                store(vT_out, hr, vT[:, :], v_out)

            n_early = PAR["conv_f_w"]
            sp.dma_start(par[:, 0:n_early], params[:, 0:n_early]).then_inc(params_in, 16)
            load(0, mem_w(0))
            for n in range(4):
                sp.dma_start(rows[:, 4 * n:4 * n + 4, 0:N_MEM],
                             k_major(memT)[:, 4 * n:4 * n + 4, :]).then_inc(mem_in[n], 16)
            load(1, mem_w(1))
            sp.dma_start(table, rel_table).then_inc(table_in, 16)
            load(2, mem_w(2))
            load(3, mem_w(3))
            load(4, mem_w(4))
            sp.wait_ge(spread_ready, 1)
            sp.dma_start(ext_dram.ap(), spread).then_inc(ext_stored, 16)
            sp.wait_ge(xhi, KT)
            sp.wait_ge(xlo, KT)
            sp.wait_ge(sums_ready, 1)
            for n in range(4):
                sp.dma_start(rows[:, 4 * n:4 * n + 4, :],
                             k_major(xT)[:, 4 * n:4 * n + 4, :]).then_inc(x_in[n], 16)
                if n < 3:
                    load(5 + n, mem_w(5 + n))
            load(U_QX, in_w(3 * D_A))
            sp.wait_ge(rg_zeroed, 1)
            for g, w in enumerate((w_rg_a, w_rg_i)):
                for b in range(2):
                    half = slice(CHUNK * b, CHUNK * (b + 1))
                    sp.dma_start(rg[half, g, :, half],
                                 w.rearrange("(t b) i j -> b i t j", b=2)[b]).then_inc(gates_in, 16)
            sp.dma_start(par[:, n_early:], params[:, n_early:]).then_inc(conv_f_in, 16)

            def store_mem_k(n):
                sp.wait_ge(normed, N_MEMK + n + 1)
                sp.dma_start(mkT_out[n], memk[:, n, :]).then_inc(mk_out, 16)

            def store_mem_v(n):
                sp.wait_ge(tile_read, HM + n + 1)
                sp.dma_start(mvT_out[n], mem_vT(n)).then_inc(mv_out[n % 2], 16)

            for n in range(3):
                store_mem_k(n)
            load(U_QX + 1, in_w(3 * D_A + D_M))
            store_mem_k(3)
            for n in range(HM):
                store_mem_v(n)
            sp.wait_ge(ext_stored, 16)
            sp.dma_start(skew_dram.ap(), bass.AP(ext_dram, P - 1, [[EXT, HA], [-1, P], [1, SEQ]])
                         ).then_inc(skew_stored, 16)
            for m in range(1, HM):
                for n in range(2):
                    load(U_QX + 2 * m + n, in_w(3 * D_A + n * D_M + m * P))
                if m >= 1:
                    m_past(m - 1)
            sp.wait_ge(skew_stored, 16)

            def period(h, hr, i=0):
                u, more = U_HEAD + PER_H * h, 2 * PER_H * i
                load(u, in_w(hr * P), more)
                if h >= 1:
                    head_loads(h - 1, hr - 1, 2 * PER_A * i, 2 * TILES * i)
                if h >= 2:
                    store_v(h - 2, hr - 2, 2 * i)
                load(u + 1, in_w(hr * P + D_A), more)
                if h == 0:
                    m_past(HM - 1)
                load(u + 2, in_w(hr * P + 2 * D_A), more)
                if h >= 1:
                    store_k(h - 1, hr - 1, 2 * i)

            period(0, 0)
            period(1, 1)
            with sp.Fori(0, 3) as i:
                period(2, 2 * i + 2, i)
                period(3, 2 * i + 3, i)
            load(U_GB, in_w(3 * D_A + D_M + D_RNN))
            head_loads(HA - 1, HA - 1)
            store_v(HA - 2, HA - 2)
            load(U_GB + 1, in_w(3 * D_A + D_M + D_RNN + P))
            load(U_GB + 2, in_w(3 * D_A + D_M + D_RNN + 2 * P))
            store_k(HA - 1, HA - 1)
            load(U_GB + 3, in_w(3 * D_A + D_M + D_RNN + 3 * P))
            store_v(HA - 1, HA - 1)

            def out_w(m):
                return k_major(w_out)[:, :, bass.ds(m * P, P)]

            load(U_OUT, out_w(0))
            load(U_OUT + 1, out_w(1))
            load(U_OUT + 2, out_w(2))
            sp.wait_ge(mixed, RT)
            sp.dma_start(b_conv_out, b_last[:]).then_inc(small_out, 16)
            sp.dma_start(b_h_out, h_last[:]).then_inc(small_out, 16)
            load(U_OUT + 3, out_w(3))
            sp.wait_ge(xhi, 4 * KT)
            sp.wait_ge(xlo, 4 * KT)
            for n in range(4):
                sp.dma_start(rows[:, 4 * n:4 * n + 4, :],
                             k_major(xT)[:, 4 * n:4 * n + 4, :]).then_inc(x_again[n], 16)
            with sp.Fori(0, 3) as i:
                for n in range(4):
                    load(U_OUT + 4 + n, out_w(4 * i + 4 + n), 4 * i)

            def up_w(g, j, gate):
                return k_major(w_up)[:, :, bass.ds((g * GROUP + j) * P + gate * D_FF, P)]

            def down_w(g, q):
                n = DOWN_TILES * P
                return k_major(w_down)[:, bass.ds(g * GROUP, GROUP), q * n:(q + 1) * n]

            for j in range(GROUP):
                load(U_FF + 2 * j, up_w(0, j, 0))
                load(U_FF + 2 * j + 1, up_w(0, j, 1))
            with sp.Fori(0, NG - 1) as i:
                u = U_LOOP
                for j in range(GROUP):
                    for gate in range(2):
                        load(u, up_w(i + 1, j, gate), FF_PER * i)
                        u += 1
                    if j == 0:
                        for q in range(DOWN):
                            load(u, down_w(i, q), FF_PER * i)
                            u += 1
            for q in range(DOWN):
                load(U_LAST + q, down_w(NG - 1, q))
            sp.wait_ge(up_ready, 2 * FT)
            sp.dma_start(f_conv_out, f_last[:]).then_inc(small_out, 16)
            ends = [DOWN_TILES * q for q in range(DOWN)] + list(range(KT - DOWN_TILES + 2, KT + 1))
            for a, b in zip(ends, ends[1:]):
                sp.wait_ge(tile_read, tiles_through(U_LAST - 1) + b)
                sp.dma_start(k_major(yT)[:, a:b, :], rows[:, a:b, :]).then_inc(y_out, 16)
            sp.wait_ge(mk_out, 16 * HM)
            for n in range(2):
                sp.wait_ge(mv_out[n], 16 * 2)
            sp.wait_ge(k_out, 16 * HA)
            sp.wait_ge(v_out, 16 * HA)
            sp.wait_ge(small_out, 16 * 3)
            sp.wait_ge(y_out, 16 * (len(ends) - 1))

        @block.gpsimd
        def _(pool):
            chain = Chain(pool, pool_step)
            nc.gpsimd.memset(mean_rows[:], 1.0 / D).then_inc(consts, 1)
            nc.gpsimd.memset(z[:, 0, 0:P], 1.0 / P).then_inc(consts, 1)
            nc.gpsimd.memset(eps[:], EPS).then_inc(consts, 1)
            nc.gpsimd.memset(zero[:], 0.0).then_inc(consts, 1)
            chain.link(nc.gpsimd.memset(ident[:], 0.0))
            nc.gpsimd.affine_select(out=ident[:], in_=ident[:], compare_op=ALU.not_equal, fill=1.0,
                                    base=0, pattern=[[-1, P]], channel_multiplier=1
                                    ).then_inc(consts, 1)
            nc.gpsimd.memset(rg[:], 0.0).then_inc(rg_zeroed, 1)
            nc.gpsimd.memset(xb[:, 0:CB - 1], 0.0).then_inc(consts, 1)

            def sum_squares(total, square, width, ready, squared=[]):
                for k in range(KT):
                    ready(k)
                    tile = rows[:, k, 0:width]
                    if k == 0:
                        chain.link(nc.gpsimd.tensor_tensor(total[:, 0:width], tile, tile, ALU.mult))
                        continue
                    if k < KT - len(squared):
                        term = square[:, 0:width]
                        chain.link(nc.gpsimd.tensor_tensor(term, tile, tile, ALU.mult))
                    else:
                        term = squared[k - KT]
                    add = nc.gpsimd.tensor_tensor(total[:, 0:width], total[:, 0:width], term, ALU.add)
                    if k < KT - 1:
                        chain.link(add)
                add.then_inc(sums_ready, 1)

            def mem_ready(k):
                if k < KT - len(mem_squares):
                    pool.wait_ge(mem_in[k // 4], 16)
                else:
                    pool.wait_ge(row_squares, k - (KT - len(mem_squares)) + 1)

            sum_squares(sum0, sq0, N_MEM, mem_ready, mem_squares)
            pool.wait_ge(sums_ready, 1)
            pool.wait_ge(means_ready, N_MEMROWS + 1)

            def x_ready(k):
                if k < KT - len(x_squares):
                    pool.wait_ge(x_in[k // 4], 16)
                else:
                    pool.wait_ge(row_squares, len(mem_squares) + k - (KT - len(x_squares)) + 1)

            sum_squares(sum0, sq0, ROWS, x_ready, x_squares)

            def mask(h, i=0):
                pool.wait_ge(bias_in[h % 2], 16 * (h // 2 + 1) + 16 * i)
                apart(pool, i)
                nc.gpsimd.memset(bias[0:CHUNK, h % 2, SEQ - CHUNK:SEQ], MASKED).then_inc(bias_masked, 1)

            mask(0)
            with pool.Fori(0, 3) as i:
                mask(1, i)
                mask(2, i)
            mask(HA - 1)

            pool.wait_ge(flip_read, flips_before(HM + HA))
            pool.wait_ge(mixed, RT)
            pool.wait_ge(k_out, 16 * HA)
            pool.wait_ge(v_out, 16 * HA)
            pool.wait_ge(xlo, 4 * KT)
            sum_squares(sum1, sq1, ROWS, lambda k: pool.wait_ge(tile_read, U_OUT + k + 1))
            for n in range(2):
                nc.gpsimd.memset(upb[n][:, 0:CF - 1], 0.0).then_inc(edges, 1)

        @block.scalar
        def _(act):
            def hi(u, more=0, tiles=0):
                if u:
                    act.wait_ge(hi_split, u + more)
                act.wait_ge(raw_loaded[u % 2], 16 * (u // 2 + 1) + 8 * more)
                if u >= 2:
                    act.wait_ge(tile_ready, tiles_through(u - 2) + tiles)
                nc.scalar.copy(wh[:, u % 2, :], raw[:, u % 2, :]).then_inc(hi_split, 1)

            def split_rows(gain, first, end, ready, at=11, between=None, tiles=range(KT)):
                for k in tiles:
                    ready(k)
                    src, dst = rows[:, k, first:end], xh[:, k, first:end]
                    if gain is None:
                        nc.scalar.copy(dst, src).then_inc(xhi, 1)
                    else:
                        nc.scalar.mul(dst, src, col(gain, k)).then_inc(xhi, 1)
                    if between and k == at:
                        between()

            def square(n, u, more=0, tiles=0, width=ROWS):
                act.wait_ge(tile_read, u + 1 + tiles)
                act.wait_ge(means_ready, n + more)
                src, dst = (z[:], sq_high[:]) if width == ROWS else \
                    (z[:, 0, 0:width], sq[:, 0, 0:width])
                nc.scalar.activation(dst, src, ACT.Square).then_inc(squares, 1)

            def root(n, more=0, width=ROWS, out=sd):
                act.wait_ge(means_ready, n + 1 + more)
                if n > 0:
                    act.wait_ge(normed, n + more)
                if width == ROWS:
                    dst, src = out[:], means[:, :, 0:HALF]
                else:
                    dst, src = out[:, 0, 0:width], means[:, 0, 0:width]
                nc.scalar.activation(dst, src, ACT.Sqrt, bias=eps[:]).then_inc(roots_ready, 1)

            def exps(a, t, more=0):
                act.wait_ge(logits_ready, TILES * a + t + 1 + TILES * more)
                n, w = (P if t < Q_TILES else DEC), keys(a, t)
                nc.scalar.activation(prob[t][0:n, 0:w], prob[t][0:n, 0:w], ACT.Exp,
                                     bias=row_neg[0:n, t:t + 1],
                                     accum_out=row_sum[0:n, t:t + 1]).then_inc(exps_ready, 1)

            def read_prob(a, t, more=0):
                w = flips_before(a) + (2 if a >= HM else 0) + t
                act.wait_ge(flip_ready, w + 1 + PER_A * more)
                at = probT_at(a, t)
                if t < Q_TILES:
                    n = keys(a, t)
                    nc.scalar.copy(probT[:, at:at + n], flip[:, 0:n]).then_inc(flip_read, 1)
                elif a < HM:
                    nc.scalar.copy(probT[:, at:at + 2 * DEC], flip[:, 0:2 * DEC]).then_inc(flip_read, 1)
                else:
                    chain.link(nc.scalar.copy(probT[:, at:at + DEC], flip[:, 0:DEC]))
                    nc.scalar.copy(probT[0:DEC, at + DEC:at + 2 * DEC],
                                   flip[0:DEC, DEC:2 * DEC]).then_inc(flip_read, 1)

            def read_v(h, s, more=0):
                act.wait_ge(flip_ready, flips_before(HM + h) + s + 1 + PER_A * more)
                if s == 0:
                    nc.scalar.copy(v_rows[:, 0:Q_TILES, :],
                                   flip.rearrange("p (t n) -> p t n", n=P)).then_inc(flip_read, 1)
                else:
                    nc.scalar.copy(v_rows[0:DEC, Q_TILES, :], flip[0:DEC, 0:P]).then_inc(flip_read, 1)

            def read_output(a, s, slot, more=0):
                w = flips_before(a + 1) - 2 + s
                act.wait_ge(flip_ready, w + 1 + PER_A * more)
                n, at = (SEQ, 0) if s == 0 else (DEC, SEQ)
                dst = rows[:, slot, at:at + n] if isinstance(slot, int) else \
                    rows[:, bass.ds(slot, 1), at:at + n].rearrange("p o n -> p (o n)")
                nc.scalar.copy(dst, flip[:, 0:n]).then_inc(flip_read, 1)

            def memory_head(m, beat):
                if beat == 8:
                    read_output(m, 1, HA + m)
                if beat == 7:
                    read_output(m, 0, HA + m)
                if 2 <= beat < 2 + TILES:
                    read_prob(m, beat - 2)
                if beat < TILES:
                    exps(m, beat)

            def band_head(h, hr, beat, i=0):
                a = HM + h
                if beat in (1, 2):
                    read_v(h, beat - 1, 2 * i)
                if 3 <= beat < 3 + TILES:
                    read_prob(a, beat - 3, 2 * i)
                if beat in (8, 9):
                    read_output(a, beat - 8, hr, 2 * i)
                if beat < TILES:
                    exps(a, beat, 2 * i)

            def recurrence(j, beat, last=False):
                if (beat == 2) != last:
                    return
                if beat == 0:
                    act.wait_ge(xb_ready, j + 1)
                    w, b = col("conv_b_w", (CB - 1) * RT + j), col("conv_b_b", j)
                    chain.link(nc.scalar.activation(xc[:, 0:SEQ], xb[:, CB - 1:CB - 1 + SEQ],
                                                    ACT.Identity, bias=b, scale=w))
                    at = SEQ + 2 * (CB - 1)
                    nc.scalar.activation(xc[:, SEQ:ROWS], xb[:, at:at + DEC], ACT.Identity,
                                         bias=b, scale=w).then_inc(b_tap, 1)
                if beat in (2, 3):
                    n = beat - 2
                    act.wait_ge(gate_ready, 2 * j + n + 1)
                    nc.scalar.activation(halves((ga, gi)[n]), means[:, :, 0:HALF], ACT.Sigmoid,
                                         bias=col(("b_rg_a", "b_rg_i")[n], j)).then_inc(gate_open, 1)
                if beat == 4:
                    act.wait_ge(lam_ready, 1)
                    act.wait_ge(gate_open, 2 * j + 1)
                    chain.link(nc.scalar.activation(dec, ga, ACT.Exp, scale=lam[:, 6, j:j + 1]))
                    nc.scalar.activation(tan, ga, ACT.Tanh, scale=lam[:, 0, j:j + 1]
                                         ).then_inc(decay_ready, 1)
                if beat == 5:
                    act.wait_ge(ratio_ready, j + 1)
                    nc.scalar.activation(tan, tan, ACT.Sqrt, bias=zero[:]).then_inc(scale_ready, 1)

            def head_norm(beat, h, q_or_k, i=0):
                n = N_HEAD + 2 * h + q_or_k
                if beat == 0:
                    square(n, U_HEAD + PER_H * h + q_or_k, 4 * i, 2 * PER_H * i)
                else:
                    root(n, 4 * i)

            chain = Chain(act, act_step)
            act.wait_ge(consts, 6)
            act.wait_ge(params_in, 16)
            act.wait_ge(prepared, 1)
            nc.scalar.activation(lam[:, 1, :], lam[:, 0, :], ACT.Exp, scale=-1.0).then_inc(lam_exp, 1)
            hi(0)
            split_rows("g_mem", 0, N_MEM, lambda k: act.wait_ge(mem_in[k // 4], 16))
            hi(1)
            for n, term in enumerate(mem_squares):
                nc.scalar.activation(term, rows[:, KT - len(mem_squares) + n, 0:N_MEM], ACT.Square
                                     ).then_inc(row_squares, 1)

            def read_mem_v(n):
                act.wait_ge(flip_ready, n + 1)
                nc.scalar.copy(memv[:, n], flip[:, 0:N_MEM].rearrange("p (c n) -> p c n", c=2)
                               ).then_inc(flip_read, 1)

            def x_ready(k):
                act.wait_ge(x_in[k // 4], 16)

            hi(2)
            hi(3)
            root(N_MEMROWS, width=N_MEM)
            for u in range(3, U_QX):
                hi(u + 1)
                for what, n in mem_steps(u):
                    if what == "k":
                        square(N_MEMK + n, n, width=N_MEM)
                        root(N_MEMK + n, width=N_MEM)
                tiles = x_early(u)
                split_rows("g_attn", N_MEM, ROWS, x_ready, tiles=tiles[:6])
                if u in (6, 7):
                    read_mem_v(u - 6)
                split_rows("g_attn", N_MEM, ROWS, x_ready, tiles=tiles[6:])

            for n, term in enumerate(x_squares):
                nc.scalar.activation(term, rows[:, KT - len(x_squares) + n, :], ACT.Square
                                     ).then_inc(row_squares, 1)

            def x_rest_ready(k):
                if k == 0:
                    act.wait_ge(rows_used, 1)
                if k == KT // 2:
                    act.wait_ge(tile_ready, U_QX)

            split_rows("g_attn", 0, N_MEM, x_rest_ready, tiles=range(KT // 4))
            read_mem_v(2)
            split_rows("g_attn", 0, N_MEM, x_rest_ready, 11, lambda: hi(U_QX + 1), range(KT // 4, KT))
            read_mem_v(HM - 1)
            for m in range(HM):
                u = U_QX + 2 * m
                if m >= 1:
                    hi(u + 1)
                    for beat in range(4):
                        if beat == 0 and m >= 2:
                            memory_head(m - 2, 8)
                        recurrence(m - 1, beat)
                        memory_head(m - 1, beat)
                        recurrence(m - 1, beat, True)
                if m == 0:
                    root(N_XROWS)
                    hi(u + 2)
                square(N_QM + m, u)
                for beat in range(4, 8):
                    if beat == 5 and m >= 1:
                        hi(u + 2)
                    if m >= 1:
                        if beat != 5:
                            recurrence(m - 1, beat)
                        memory_head(m - 1, beat)
                    if beat == 5:
                        root(N_QM + m)
                        if m >= 1:
                            recurrence(m - 1, beat)

            for beat in range(12):
                if beat in (4, 8):
                    head_norm(0, 0, beat // 4 - 1)
                if beat in (0, 5, 8):
                    hi(U_HEAD + 1 + beat // 4)
                if beat == 0:
                    memory_head(HM - 2, 8)
                if beat < 9:
                    if beat != 5:
                        recurrence(HM - 1, beat)
                    memory_head(HM - 1, beat)
                    recurrence(HM - 1, beat, True)
                    if beat == 5:
                        head_norm(1, 0, 0)
                        recurrence(HM - 1, beat)
                if beat == 9:
                    head_norm(1, 0, 1)

            def period(h, hr, i=0):
                u, more = U_HEAD + PER_H * h, 2 * PER_H * i
                for beat in range(12):
                    if beat in (4, 8):
                        head_norm(0, h, beat // 4 - 1, i)
                    if beat % 4 == 0:
                        hi(u + 1 + beat // 4, more, more)
                    band_head(h - 1, hr - 1, beat, i)
                    if beat in (5, 9):
                        head_norm(1, h, beat // 4 - 1, i)

            period(1, 1)
            with act.Fori(0, 3) as i:
                chain.enter(i, 2)
                period(2, 2 * i + 2, i)
                period(3, 2 * i + 3, i)
                chain.leave(3)

            def gelu_gate(j):
                act.wait_ge(tile_read, U_GB + j + 1)
                nc.scalar.activation(z[:], z[:], ACT.Gelu_apprx_tanh).then_inc(g_gelu, 1)

            for beat in range(12):
                if beat % 4 == 0:
                    hi(U_GB + 1 + beat // 4)
                band_head(HA - 1, HA - 1, beat)
                if beat in (7, 11):
                    gelu_gate(beat // 4 - 1)
            hi(U_OUT)
            gelu_gate(2)

            def o_ready(k):
                if k == 0:
                    act.wait_ge(rows_used, 2)
                    act.wait_ge(flip_read, flips_before(HM + HA))
                if k == KT // 2:
                    act.wait_ge(tile_ready, U_OUT)
                    gelu_gate(3)
                if k >= HA + HM:
                    act.wait_ge(mixed, k - HA - HM + 1)

            split_rows(None, 0, ROWS, o_ready, 11, lambda: hi(U_OUT + 1))
            for n in range(1, 4):
                hi(U_OUT + n + 1)
            with act.Fori(0, 2) as i:
                for n in range(4):
                    hi(U_OUT + 5 + n, 4 * i, 4 * i)
            for u in range(U_OUT + 13, U_FF + 1):
                hi(u)

            def x1_ready(k):
                act.wait_ge(tile_read, U_OUT + k + 1)
                if k == 0:
                    act.wait_ge(rows_used, 2 + 3)
                if k == KT // 2:
                    act.wait_ge(tile_ready, U_FF)

            split_rows("g_ffn", 0, ROWS, x1_ready, 11, lambda: hi(U_FF + 1))
            act.wait_ge(conv_f_in, 16)
            root(N_X1ROWS, out=sd1)

            def feed(g0, i=0, gr=0):
                order = ff_order(g0)
                u = U_FF if g0 == 0 else U_LOOP
                for pos, (kind, j, gate) in enumerate(order):
                    if g0 or pos:
                        hi(u + pos + 1, FF_PER * i, FF_TILES * i)
                    last = order[pos - 1] if pos else ("up", GROUP - 1, 1)
                    if pos or g0:
                        gg, ii = (g0, i) if pos else (g0 - 1, i)
                        up_tile(gg, ii, gr if pos else gr - 1, last, pos == 2 and g0)
                    if g0 and pos == 2 + DOWN:
                        write_h(g0, i, 0)

            def up_tile(g, i, gr, unit, held):
                kind, j, gate = unit
                if kind == "down":
                    return
                e = 2 * GROUP * g + 2 * j + gate
                act.wait_ge(up_ready, e + 1 + 2 * GROUP * i)
                done = GROUP * g + j
                if done or not isinstance(i, int):
                    act.wait_ge(h_ready if gate else h_lo, done + GROUP * i)
                tile = gate * FT + GROUP * gr + j
                nc.scalar.activation(cv[gate][:], upb[gate][:, CF - 1:up_w], ACT.Identity,
                                     bias=col("conv_f_b", tile),
                                     scale=col("conv_f_w", tile + (CF - 1) * 2 * FT)
                                     ).then_inc(f_tap, 1)
                if gate:
                    act.wait_ge(gate_conv, done + 1 + GROUP * i)
                    nc.scalar.activation(cv[1][:], cv[1][:], ACT.Gelu_apprx_tanh).then_inc(gate_gelu, 1)
                    if not held:
                        write_h(g, i, j)

            def write_h(g, i, j):
                act.wait_ge(h_ready, GROUP * g + j + 1 + GROUP * i)
                if g:
                    act.wait_ge(tile_ready, tiles_through(U_LOOP + 1 + DOWN + FF_PER * (g - 1))
                                + FF_TILES * i)
                chain.link(nc.scalar.copy(hh[:, j, 0:SEQ], cv[0][:, 0:SEQ]))
                nc.scalar.copy(hh[:, j, SEQ:ROWS], cv[0][:, SEQ + CF - 1:]).then_inc(h_hi, 1)

            feed(0)
            with act.Fori(0, NG - 1) as i:
                chain.enter(i, GROUP)
                feed(1, i, i + 1)
                chain.leave(NG - 1)
            up_tile(NG - 1, 0, NG - 1, ("up", GROUP - 1, 1), False)
            hi(U_LAST + 1)
            for q in range(1, DOWN - 1):
                hi(U_LAST + q + 1)

        @block.vector
        def _(dve):
            chain = Chain(dve, dve_step)
            link = chain.link

            def lo(u, more=0):
                if u:
                    dve.wait_ge(lo_split, u + more)
                dve.wait_ge(hi_split, u + 1 + more)
                nc.vector.tensor_tensor(wl[:, u % 2, :], raw[:, u % 2, :],
                                        wh[:, u % 2, :].bitcast(F32), ALU.subtract).then_inc(lo_split, 1)

            def split_rows(count, gain, first, end, at=11, between=None, tiles=range(KT)):
                for k in tiles:
                    dve.wait_ge(xhi, count + k + 1)
                    src, high, dst = (t[:, k, first:end] for t in (rows, xh, xl))
                    if gain is None:
                        ins = nc.vector.tensor_tensor(dst, src, high.bitcast(F32), ALU.subtract)
                    else:
                        ins = nc.vector.scalar_tensor_tensor(dst, src, col(gain, k), high.bitcast(F32),
                                                             ALU.mult, ALU.subtract)
                    ins.then_inc(xlo, 1)
                    if between and k == at:
                        between()

            def psum(t):
                if t < U_QX:
                    return mem_bank(t)
                return slots[t % 2][:, :, 0:HALF]

            def read_z(u, n, more=0, norms=0, width=ROWS):
                dve.wait_ge(normed, n + norms)
                dve.wait_ge(tile_ready, u + 1 + more)
                if width == ROWS:
                    dst, src, r = z[:], psum(u), rstd[:]
                else:
                    dst, src, r = z[:, 0, 0:width], psum(u), rstd[:, 0, 0:width]
                nc.vector.tensor_tensor(dst, src, r, ALU.mult).then_inc(tile_read, 1)

            def read_v(u, v, more=0, more_v=0, width=ROWS):
                before = v if v >= HM else v - 1
                if v > HM:
                    dve.wait_ge(v_out, 16 * (v - HM) + 16 * more_v)
                if v == HM:
                    for n in range(2):
                        dve.wait_ge(mv_out[n], 16 * 2)
                if 2 <= v < HM:
                    dve.wait_ge(mv_out[v % 2], 16 * (v // 2))
                if before > 0:
                    flips = before if v <= HM else flips_before(v - 1) + 2
                    dve.wait_ge(flip_ready, flips + PER_A * more_v)
                dve.wait_ge(tile_ready, u + 1 + more)
                if width == ROWS:
                    dst, src, r = halves(vT[:, :]), psum(u), rstd[:]
                else:
                    dst, src, r = mem_vT(v), psum(u), rstd[:, 0, 0:width]
                nc.vector.tensor_tensor(dst, src, r, ALU.mult).then_inc(tile_read, 1)

            def normalise(n, dst, gain, more=0, width=ROWS):
                dve.wait_ge(roots_ready, n + 1 + more)
                if width == ROWS:
                    r, src = sd[:], z[:]
                    dst = halves(dst)
                else:
                    r, src = sd[:, 0, 0:width], z[:, 0, 0:width]
                link(nc.vector.reciprocal(r, r))
                nc.vector.scalar_tensor_tensor(dst, src, gain, r, ALU.mult, ALU.mult).then_inc(normed, 1)

            def square_low(u, count, more=0, norms=0):
                dve.wait_ge(tile_read, u + 1 + more)
                link(nc.vector.tensor_tensor(sd[:], z[:], z[:], ALU.mult))
                dve.wait_ge(squares, HM + count + 1 + norms)
                nc.vector.tensor_tensor(sq_low[:], sd[:], sq_high[:].bitcast(F32), ALU.subtract).then_inc(squares_low, 1)

            def row_factor(n, src, width=ROWS):
                dve.wait_ge(roots_ready, n + 1)
                dst, src = (rstd[:], src[:]) if width == ROWS else \
                    (rstd[:, 0, 0:width], src[:, 0, 0:width])
                nc.vector.reciprocal(dst, src).then_inc(normed, 1)
                dve.wait_ge(normed, n + 1)

            def logits(a, t, more=0):
                n, w = (P if t < Q_TILES else DEC), keys(a, t)
                dve.wait_ge(scores_ready, TILES * a + t + 1 + TILES * more)
                if a >= 1:
                    before = flips_before(a - 1) + (2 if a > HM else 0) + t + 1
                    dve.wait_ge(flip_ready, before + PER_A * more)
                if a < HM:
                    add = zero[0:n, 0:1].to_broadcast([n, w])
                else:
                    h = a - HM
                    if t == 0:
                        dve.wait_ge(bias_masked, h + 1 + more)
                    first = SEQ - w if t < Q_TILES else Q_TILES * P - PAST - P
                    add = bias[0:n, h % 2, first:first + w]
                apart(dve, more)
                link(nc.vector.tensor_tensor_reduce(
                    out=prob[t][0:n, 0:w], in0=scores[0:n, 0:w], in1=add, scale=1.0, scalar=-3e38,
                    op0=ALU.add, op1=ALU.max, accum_out=row_max[0:n, t:t + 1]))
                nc.vector.tensor_scalar(row_neg[0:n, t:t + 1], row_max[0:n, t:t + 1], -1.0, None,
                                        ALU.mult).then_inc(logits_ready, 1)

            def probs(a, t, more=0):
                n, w = (P if t < Q_TILES else DEC), keys(a, t)
                dve.wait_ge(exps_ready, TILES * a + t + 1 + TILES * more)
                link(nc.vector.reciprocal(row_inv[0:n, t:t + 1], row_sum[0:n, t:t + 1]))
                nc.vector.tensor_scalar(prob[t][0:n, 0:w], prob[t][0:n, 0:w], row_inv[0:n, t:t + 1],
                                        None, ALU.mult).then_inc(probs_ready, 1)

            def head(a, beat, more=0):
                if beat < TILES:
                    logits(a, beat, more)
                if 1 <= beat <= TILES:
                    probs(a, beat - 1, more)

            def recurrence(j, beat):
                def tap(k):
                    return col("conv_b_w", k * RT + j)

                if beat == 0:
                    u = U_QX + 2 * j + 1
                    dve.wait_ge(tile_ready, u + 1)
                    src = psum(u)
                    nc.vector.tensor_tensor(
                        xb[:, CB - 1:CB - 1 + HALF], src[:, 0, :], rstd[:, 0, :], ALU.mult)
                    nc.vector.tensor_tensor(
                        xb[:, CB - 1 + HALF:CB - 1 + SEQ], src[:, 1, 0:BODY], rstd[:, 1, 0:BODY], ALU.mult)
                    at = SEQ + 2 * (CB - 1)
                    nc.vector.tensor_tensor(xb[:, at:at + DEC], src[:, 1, BODY:HALF],
                                            rstd[:, 1, BODY:HALF], ALU.mult).then_inc(tile_read, 1)
                    dve.wait_ge(tile_read, u + 1)
                    past_b = par[:, PAR["past_b"] + j * (CB - 1):PAR["past_b"] + (j + 1) * (CB - 1)]
                    nc.vector.tensor_copy(xb[:, SEQ + CB - 1:at], past_b)
                    nc.vector.tensor_copy(b_last[:, j, 0:CB - 1], xb[:, SEQ:SEQ + CB - 1])
                    nc.vector.tensor_copy(b_last[:, j, CB - 1:], xb[:, at + DEC - CB + 1:at + DEC]
                                          ).then_inc(xb_ready, 1)
                if beat == 1:
                    dve.wait_ge(b_tap, j + 1)
                    dve.wait_ge(xb_ready, j + 1)
                    for k in range(CB - 2, -1, -1):
                        at = SEQ + CB - 1 + k
                        nc.vector.scalar_tensor_tensor(xc[:, 0:SEQ], xb[:, k:k + SEQ], tap(k),
                                                       xc[:, 0:SEQ], ALU.mult, ALU.add)
                        ins = nc.vector.scalar_tensor_tensor(xc[:, SEQ:ROWS], xb[:, at:at + DEC],
                                                             tap(k), xc[:, SEQ:ROWS], ALU.mult, ALU.add)
                        if k:
                            link(ins)
                    ins.then_inc(conv_ready, 1)
                if beat == 4:
                    dve.wait_ge(gate_open, 2 * j + 2)
                    link(nc.vector.tensor_tensor(gi, gi, xc, ALU.mult))
                if beat == 5:
                    dve.wait_ge(decay_ready, j + 1)
                    link(nc.vector.tensor_tensor(ga, dec, dec, ALU.mult))
                    nc.vector.scalar_tensor_tensor(tan, ga, 1.0, tan, ALU.add, ALU.mult
                                                   ).then_inc(ratio_ready, 1)
                if beat == 6:
                    dve.wait_ge(scale_ready, j + 1)
                    link(nc.vector.tensor_tensor(gi, gi, tan, ALU.mult))
                    out = rows[:, HA + HM + j, :]
                    nc.vector.tensor_tensor_scan(out[:, 0:SEQ], dec[:, 0:SEQ], gi[:, 0:SEQ], 0.0,
                                                 ALU.mult, ALU.add)
                    link(nc.vector.tensor_tensor_scan(out[:, SEQ:ROWS], dec[:, SEQ:ROWS],
                                                      gi[:, SEQ:ROWS], col("h0", j), ALU.mult, ALU.add))
                    nc.vector.tensor_copy(h_last[:, j, 0:1], out[:, SEQ - 1:SEQ])
                    link(nc.vector.tensor_copy(h_last[:, j, 1:2], out[:, ROWS - 1:ROWS]))

            dve.wait_ge(consts, 6)
            dve.wait_ge(params_in, 16)
            v = nc.vector
            raw_lam = par[:, PAR["lam"]:PAR["lam"] + RT]
            L = [lam[:, n, :] for n in range(7)]
            link(v.tensor_scalar(L[2], raw_lam, -1.0, None, ALU.mult))
            link(v.tensor_tensor(L[0], L[2], raw_lam, ALU.max))
            v.tensor_scalar(L[2], L[2], 0.0, None, ALU.max)
            v.tensor_copy(mean_head[:], z[:, 0, 0:P])
            v.tensor_scalar(scale_q[:, 0:1], col("g_q_a"), P ** -0.5, None, ALU.mult)
            v.tensor_scalar(scale_q[:, 1:2], col("g_q_m"), P ** -0.5, None, ALU.mult).then_inc(prepared, 1)

            lo(0)
            split_rows(0, "g_mem", 0, N_MEM)
            lo(1)
            dve.wait_ge(lam_exp, 1)
            link(v.tensor_scalar(L[3], L[1], 2.0, None, ALU.add))
            link(v.reciprocal(L[3], L[3]))
            link(v.tensor_tensor(L[4], L[1], L[3], ALU.mult))
            link(v.tensor_tensor(L[5], L[4], L[4], ALU.mult))
            link(v.tensor_scalar(L[3], L[5], 1.0 / 15, 1.0 / 13, ALU.mult, ALU.add))
            for n in (11, 9, 7, 5, 3, 1):
                link(v.tensor_tensor(L[3], L[3], L[5], ALU.mult))
                link(v.tensor_scalar(L[3], L[3], 1.0 / n, None, ALU.add))
            link(v.tensor_tensor(L[3], L[3], L[4], ALU.mult))
            link(v.scalar_tensor_tensor(L[3], L[3], 2.0, L[2], ALU.mult, ALU.add))
            v.tensor_scalar(L[6], L[3], -8.0, None, ALU.mult)
            v.tensor_scalar(L[0], L[3], 8.0, None, ALU.mult).then_inc(lam_ready, 1)
            dve.wait_ge(table_in, 16)
            flat = Q_TILES * P - 1 - REL
            v.tensor_copy(spread[:, 0:flat], table[:, 2 * REL:2 * REL + 1].to_broadcast([HA, flat]))
            v.tensor_copy(spread[:, flat:EXT], table[:, 2 * REL:2 * REL - (EXT - flat):-1]
                          ).then_inc(spread_ready, 1)

            lo(2)
            lo(3)
            row_factor(N_MEMROWS, sd, N_MEM)
            for u in range(3, U_QX):
                for step, (what, n) in enumerate(mem_steps(u)):
                    if what == "k":
                        read_z(n, N_MEMK + n, width=N_MEM)
                    else:
                        read_v(HM + n, n, width=N_MEM)
                    if step == 0:
                        lo(u + 1)
                    if what == "k":
                        normalise(N_MEMK + n, memk[:, n, :], col("g_k_m"), width=N_MEM)
                split_rows(KT, "g_attn", N_MEM, ROWS, tiles=x_early(u))
            split_rows(2 * KT, "g_attn", 0, N_MEM, tiles=range(KT // 4))
            read_v(U_QX - 1, HM - 1, width=N_MEM)
            split_rows(2 * KT, "g_attn", 0, N_MEM, 11, lambda: lo(U_QX + 1), range(KT // 4, KT))
            for m in range(HM):
                u = U_QX + 2 * m
                if m >= 1:
                    for beat in range(4):
                        recurrence(m - 1, beat)
                        if beat == 0:
                            lo(u + 1)
                        head(m - 1, beat)
                if m == 0:
                    row_factor(N_XROWS, sd)
                read_z(u, N_QM + m)
                square_low(u, m)
                if m == 0:
                    lo(u + 2)
                for beat in range(4, 8):
                    if beat == 6:
                        normalise(N_QM + m, q_m[m % 2], scale_q[:, 1:2])
                    if m >= 1:
                        recurrence(m - 1, beat)
                        head(m - 1, beat)
                        if beat == 5:
                            lo(u + 2)

            def period(h, i=0):
                u, more, a = U_HEAD + PER_H * h, 2 * PER_H * i, HM + h - 1
                for beat in range(12):
                    if beat in (4, 8):
                        qk = beat // 4 - 1
                        read_z(u + qk, N_HEAD + 2 * h + qk, more, 4 * i)
                        square_low(u + qk, HM + 2 * h + qk, more, 4 * i)
                    if h == 0:
                        recurrence(HM - 1, beat)
                    if beat in ((0, 4, 8) if h else (0, 8)):
                        lo(u + 1 + beat // 4, more)
                    if beat == 0 and h >= 1:
                        read_v(u - 1, HM + h - 1, more, 2 * i)
                    if beat == 6:
                        dve.wait_ge(scores_ready, TILES * (a + 1) + 2 * TILES * i)
                        normalise(N_HEAD + 2 * h, qT[:, :], scale_q[:, 0:1], 4 * i)
                    if beat == 10:
                        if h >= 1:
                            dve.wait_ge(k_out, 16 * h + 32 * i)
                        normalise(N_HEAD + 2 * h + 1, kT[:, :], col("g_k_a"), 4 * i)
                    head(a, beat, 2 * i)
                    if h == 0 and beat == 5:
                        lo(u + 2)

            period(0)
            period(1)
            with dve.Fori(0, 3) as i:
                chain.enter(i, 28)
                period(2, i)
                period(3, i)
                chain.leave(3)

            def read_g(j):
                if j == 0:
                    dve.wait_ge(normed, N_X1ROWS)
                dve.wait_ge(tile_ready, U_GB + j + 1)
                v.tensor_tensor(z[:], psum(U_GB + j), rstd[:], ALU.mult
                                ).then_inc(tile_read, 1)

            def mix_g(j):
                dve.wait_ge(g_gelu, j + 1)
                out = halves(rows[:, HA + HM + j, :])
                v.tensor_tensor(out, z[:], out, ALU.mult).then_inc(mixed, 1)
                dve.wait_ge(mixed, j + 1)

            for beat in range(12):
                if beat % 4 == 0:
                    lo(U_GB + 1 + beat // 4)
                if beat == 0:
                    read_v(U_GB - 1, HM + HA - 1)
                head(HM + HA - 1, beat)
                if beat in (6, 10):
                    read_g(beat // 4 - 1)
                if beat in (7, 11):
                    mix_g(beat // 4 - 1)
            lo(U_OUT)
            read_g(2)
            mix_g(2)

            def last_gate():
                read_g(3)
                mix_g(3)

            split_rows(3 * KT, None, 0, ROWS, KT // 2 - 1, last_gate, range(KT // 2))
            split_rows(3 * KT, None, 0, ROWS, 11, lambda: lo(U_OUT + 1), range(KT // 2, KT))

            def add_mix(m, mm, more=0):
                t = U_OUT + m
                dve.wait_ge(tile_ready, t + 1 + more)
                if isinstance(mm, int):
                    x = halves(rows[:, mm, :])
                else:
                    x = rows[:, bass.ds(mm, 1), :].rearrange("p o (c n) -> p (o c) n", c=2)
                v.tensor_tensor(x, psum(t), x, ALU.add).then_inc(tile_read, 1)

            for m in range(3):
                lo(U_OUT + m + 2)
                if m == 0:
                    dve.wait_ge(x_again[0], 16)
                add_mix(m, m)
            for n in range(1, 4):
                dve.wait_ge(x_again[n], 16)
            with dve.Fori(0, 3) as i:
                for n in range(4):
                    lo(U_OUT + 5 + n, 4 * i)
                    add_mix(3 + n, 4 * i + 3 + n, 4 * i)
            split_rows(4 * KT, "g_ffn", 0, ROWS, tiles=range(KT // 2))
            add_mix(KT - 1, KT - 1)
            dve.wait_ge(tile_read, U_FF)
            split_rows(4 * KT, "g_ffn", 0, ROWS, 11, lambda: lo(U_FF + 1), range(KT // 2, KT))
            row_factor(N_X1ROWS, sd1)
            dve.wait_ge(conv_f_in, 16)
            dve.wait_ge(edges, 2)

            def up_tile(g, i, gr, t, unit, held):
                kind, j, gate = unit
                if kind == "down":
                    return
                e = 2 * GROUP * g + 2 * j + gate
                buf, out = upb[gate], cv[gate]
                src = slots[t % 4]
                dve.wait_ge(tile_ready, t + 1 + FF_TILES * i)
                body = buf[:, CF - 1:CF - 1 + ROWS].rearrange("p (c n) -> p c n", c=2)[:, :, 0:BODY]
                tail = buf[:, 0:up_w].rearrange("p (c n) -> p c n", c=2)[:, :, CF - 1 + BODY:]
                v.tensor_tensor(body, src[:, :, 0:BODY], rstd[:, :, 0:BODY], ALU.mult)
                v.tensor_tensor(tail, src[:, :, BODY:HALF], rstd[:, :, BODY:HALF], ALU.mult
                                ).then_inc(tile_read, 1)
                dve.wait_ge(tile_read, t + 1 + FF_TILES * i)
                tile = gate * FT + GROUP * gr + j
                n = 2 * tile + PAR["past_f"]
                past_f = par[:, n:n + 2] if isinstance(tile, int) else par[:, bass.ds(n, 2)]
                v.tensor_copy(buf[:, CF - 1 + SEQ:2 * (CF - 1) + SEQ], past_f)
                kept = f_last[:, tile, :] if isinstance(tile, int) else \
                    f_last[:, bass.ds(tile, 1), :].rearrange("p o n -> p (o n)")
                lasts = buf[:, SEQ:].rearrange("p (c n) -> p c n", c=2)[:, :, 0:CF - 1]
                v.tensor_copy(kept.rearrange("p (c n) -> p c n", c=2), lasts).then_inc(up_ready, 1)
                dve.wait_ge(f_tap, e + 1 + 2 * GROUP * i)
                dve.wait_ge(up_ready, e + 1 + 2 * GROUP * i)
                link(v.scalar_tensor_tensor(out[:], buf[:, 1:up_w - 1], col("conv_f_w", tile + 2 * FT),
                                            out[:], ALU.mult, ALU.add))
                last = v.scalar_tensor_tensor(out[:], buf[:, 0:up_w - 2], col("conv_f_w", tile),
                                              out[:], ALU.mult, ALU.add)
                if not gate:
                    link(last)
                    return
                last.then_inc(gate_conv, 1)
                dve.wait_ge(gate_gelu, GROUP * g + j + 1 + GROUP * i)
                v.tensor_tensor(cv[0][:], cv[1][:], cv[0][:], ALU.mult).then_inc(h_ready, 1)
                if not held:
                    low_h(g, i, j)

            def low_h(g, i, j):
                dve.wait_ge(h_hi, GROUP * g + j + 1 + GROUP * i)
                v.tensor_tensor(hl[:, j, 0:SEQ], cv[0][:, 0:SEQ], hh[:, j, 0:SEQ].bitcast(F32), ALU.subtract)
                v.tensor_tensor(hl[:, j, SEQ:ROWS], cv[0][:, SEQ + CF - 1:],
                                hh[:, j, SEQ:ROWS].bitcast(F32), ALU.subtract).then_inc(h_lo, 1)

            def add_down(u, q, more=0):
                t = tiles_through(u) - DOWN_TILES
                for n in range(DOWN_TILES):
                    x = halves(rows[:, DOWN_TILES * q + n, :])
                    dve.wait_ge(tile_ready, t + n + 1 + more)
                    v.tensor_tensor(x, slots[(t + n) % 4][:, :, 0:HALF], x, ALU.add).then_inc(tile_read, 1)

            def feed(g0, i=0, gr=0):
                order = ff_order(g0)
                u = U_FF if g0 == 0 else U_LOOP
                for pos, (kind, q, _) in enumerate(order):
                    if g0 or pos:
                        lo(u + pos + 1, FF_PER * i)
                    if pos or g0:
                        last = order[pos - 1] if pos else ("up", GROUP - 1, 1)
                        t = tiles_through(u + pos - 1) - 1
                        gg, rr = (g0, gr) if pos else (g0 - 1, gr - 1)
                        up_tile(gg, i, rr, t, last, pos == 2 and g0)
                    if kind == "down":
                        add_down(u + pos, q, FF_TILES * i)
                    if g0 and pos == 2 + DOWN:
                        low_h(g0, i, 0)

            feed(0)
            with dve.Fori(0, NG - 1) as i:
                chain.enter(i, 3 * GROUP)
                feed(1, i, i + 1)
                chain.leave(NG - 1)
            up_tile(NG - 1, 0, NG - 1, tiles_through(U_LAST - 1) - 1, ("up", GROUP - 1, 1), False)
            lo(U_LAST + 1)
            for q in range(DOWN):
                if 0 < q < DOWN - 1:
                    lo(U_LAST + q + 1)
                add_down(U_LAST + q, q)

        @block.tensor
        def _(pe):
            mm = nc.tensor.matmul

            def products(out, weights, high, low, first, last):
                w_high, w_low = weights
                for c, (dst, hs, ls) in enumerate(zip(out, high, low)):
                    mm(dst, w_high, hs, start=first, stop=False)
                    mm(dst, w_high, ls, start=False, stop=False)
                for c, (dst, hs) in enumerate(zip(out, high)):
                    ins = mm(dst, w_low, hs, start=False, stop=last)
                return ins

            def unit(u, between=lambda beat: None, more=0, first=None, width=ROWS, tiles=None, bank=None,
                     stage_ends=False):
                pe.wait_ge(lo_split, u + 1 + more)
                t = tiles_through(u) - 1
                tiles = more if tiles is None else tiles
                slot = slots[t % 2] if bank is None else slots[bank]
                reuse = 4 if t < U_QX or t >= U_FF + 2 else 2
                if t >= reuse:
                    pe.wait_ge(tile_read, t - reuse + 1 + tiles)
                n = [(0, width)] if width < HALF else [(0, HALF), (HALF, ROWS)]
                out = [slot[:, c, 0:b - a] for c, (a, b) in enumerate(n)]
                if width < HALF:
                    out = [mem_bank(t)]
                w = [buf[:, u % 2, :].rearrange("p (k n) -> p k n", k=KT) for buf in (wh, wl)]
                for k in range(KT):
                    if first is not None:
                        pe.wait_ge(xlo, first + k + 1)
                    ins = products(out, [x[:, k, :] for x in w], [xh[:, k, a:b] for a, b in n],
                                   [xl[:, k, a:b] for a, b in n], k == 0, k == KT - 1)
                    if k == KT // 2 - 1 and stage_ends:
                        ins.then_inc(rows_used, 1)
                    if k == KT - 1:
                        ins.then_inc(tile_ready, 1)
                    if k % 4 == 3:
                        between(k // 4)

            def mean(n, matrix, square, more=0, width=ROWS):
                if n > 0:
                    pe.wait_ge(roots_ready, n + more)
                if width < ROWS:
                    mm(means[:, 0, 0:width], matrix, square[:, 0:width],
                       start=True, stop=True).then_inc(means_ready, 1)
                    return
                for c in range(2):
                    ins = mm(means[:, c, 0:HALF], matrix, square[:, c * HALF:(c + 1) * HALF],
                             start=True, stop=True)
                ins.then_inc(means_ready, 1)

            def flat(ap):
                return ap.rearrange("p c n -> p (c n)")

            def mem_mean(m):
                pe.wait_ge(squares, m + 1)
                mean(N_MEMK + m, mean_head[:].bitcast(F32), sq[:, 0, :], width=N_MEM)

            def head_mean(n, count, more=0):
                pe.wait_ge(squares_low, count + more)
                pe.wait_ge(roots_ready, n + more)
                for c in range(2):
                    mm(means[:, c, 0:HALF], mean_head[:], sq_high[:, c, :], start=True, stop=False)
                    ins = mm(means[:, c, 0:HALF], mean_head[:], sq_low[:, c, :], start=False, stop=True)
                ins.then_inc(means_ready, 1)

            def score(a, t, more=0):
                if a or t:
                    pe.wait_ge(logits_ready, TILES * a + t + TILES * more)
                s = a % 2
                if t == 0:
                    n = N_QM + a + 1 if a < HM else N_HEAD + 2 * (a - HM) + 2
                    pe.wait_ge(normed, n + 2 * more)
                if t == Q_TILES:
                    pe.wait_ge(past_in[s], 32 * (a // 2 + 1) + 16 * more)
                q = q_m[s] if a < HM else qT[:, :]
                cached = flat(past[:, s, 0:2, :])
                if t < Q_TILES:
                    key = memk[:, a, :] if a < HM else kT[:, 0:keys(a, t)]
                    ins = mm(scores[:, 0:keys(a, t)], q[:, t * P:(t + 1) * P], key, start=True, stop=True)
                elif a < HM:
                    ins = mm(scores[0:DEC, 0:N_MEM], q[:, SEQ:ROWS], cached, start=True, stop=True)
                else:
                    mm(scores[0:DEC, 0:PAST], q[:, SEQ:ROWS], cached[:, 0:PAST], start=True, stop=True)
                    ins = mm(scores[0:DEC, PAST:PAST + DEC], q[:, SEQ:ROWS], kT[:, SEQ:ROWS],
                             start=True, stop=True)
                ins.then_inc(scores_ready, 1)

            def flip_free(w, more=0):
                if w:
                    pe.wait_ge(flip_read, w + more)

            def turn(dst, src):
                n = src.shape[0]
                return nc.tensor.transpose(dst, src, ident[0:n, 0:n])

            def flip_prob(a, t, more=0):
                w = flips_before(a) + (2 if a >= HM else 0) + t
                pe.wait_ge(probs_ready, TILES * a + t + 1 + TILES * more)
                flip_free(w, PER_A * more)
                if t < Q_TILES:
                    for c in range(keys(a, t) // P):
                        ins = turn(flip[:, c * P:(c + 1) * P], prob[t][:, c * P:(c + 1) * P])
                else:
                    apart(pe, more)
                    turn(flip[:, 0:DEC], prob[t][0:DEC, 0:P])
                    n = P if a < HM else DEC
                    ins = turn(flip[0:n, DEC:2 * DEC], prob[t][0:DEC, P:P + n])
                ins.then_inc(flip_ready, 1)

            def flip_memory(m):
                pe.wait_ge(tile_read, HM + m + 1)
                flip_free(m)
                for c in range(2):
                    ins = turn(flip[:, c * P:(c + 1) * P], mem_vT(m)[:, c * P:(c + 1) * P])
                ins.then_inc(flip_ready, 1)

            def flip_v(h, s, more=0):
                pe.wait_ge(tile_read, U_HEAD + PER_H * (h + 1) + PER_H * more)
                flip_free(flips_before(HM + h) + s, PER_A * more)
                if s == 0:
                    for t in range(Q_TILES):
                        ins = turn(flip[:, t * P:(t + 1) * P], vT[:, t * P:(t + 1) * P])
                else:
                    ins = turn(flip[0:DEC, 0:P], vT[:, SEQ:ROWS])
                ins.then_inc(flip_ready, 1)

            def output(a, s, more=0):
                flip_free(flips_before(a + 1) - 2 + s, PER_A * more)
                if s == 0:
                    for t in range(Q_TILES):
                        n = keys(a, t) // P
                        for c in range(n):
                            value = memv[:, a, c, :] if a < HM else v_rows[:, c, :]
                            at = probT_at(a, t) + c * P
                            ins = mm(flip[:, t * P:(t + 1) * P], value, probT[:, at:at + P],
                                     start=c == 0, stop=c == n - 1)
                else:
                    at = probT_at(a, Q_TILES)
                    mm(flip[:, 0:DEC], past[:, a % 2, 2, :], probT[:, at:at + DEC], start=True, stop=False)
                    if a < HM:
                        ins = mm(flip[:, 0:DEC], past[:, a % 2, 3, :], probT[:, at + DEC:at + 2 * DEC],
                                 start=False, stop=True)
                    else:
                        ins = mm(flip[:, 0:DEC], v_rows[0:DEC, Q_TILES, :],
                                 probT[0:DEC, at + DEC:at + 2 * DEC], start=False, stop=True)
                ins.then_inc(flip_ready, 1)

            def memory_head(m, beat):
                if beat < TILES:
                    score(m, beat)
                if 2 <= beat < 2 + TILES:
                    flip_prob(m, beat - 2)
                if beat == 7:
                    output(m, 0)

            def band_head(h, beat, i=0):
                a, more = HM + h, 2 * i
                if beat < TILES:
                    score(a, beat, more)
                if beat in (1, 2):
                    flip_v(h, beat - 1, more)
                if 3 <= beat < 3 + TILES:
                    flip_prob(a, beat - 3, more)
                if beat in (8, 9):
                    output(a, beat - 8, more)

            def gate(j, n):
                pe.wait_ge(conv_ready, j + 1)
                pe.wait_ge(roots_ready, N_QM + j + 1)
                if j or n:
                    pe.wait_ge(gate_open, 2 * j + n)
                for c in range(2):
                    ins = mm(means[:, c, 0:HALF], rg[:, n, j, :], xc[:, c * HALF:(c + 1) * HALF],
                             start=True, stop=True)
                ins.then_inc(gate_ready, 1)

            pe.wait_ge(consts, 6)

            def mem_between(u):
                def between(beat):
                    if u == 2 and beat == 1:
                        pe.wait_ge(sums_ready, 1)
                        mean(N_MEMROWS, mean_rows[:], sum0, width=N_MEM)
                    for n, (what, m) in enumerate(mem_steps(u)):
                        if beat != (2, 3)[n]:
                            continue
                        if what == "k":
                            mem_mean(m)
                        else:
                            flip_memory(m)
                return between

            for u in range(U_QX):
                unit(u, mem_between(u), width=N_MEM, first=0 if u == 0 else None,
                     stage_ends=u == U_QX - 1)

            pe.wait_ge(gates_in, 16 * 4)
            for m in range(HM):
                u = U_QX + 2 * m

                def q_between(beat, m=m):
                    if m == 0:
                        if beat == 2:
                            flip_memory(HM - 1)
                        if beat == 3:
                            pe.wait_ge(sums_ready, 2)
                            mean(N_XROWS, mean_rows[:], sum0)
                        return
                    if beat == 0 and m >= 2:
                        output(m - 2, 1)
                    memory_head(m - 1, beat)
                    if beat in (2, 3):
                        gate(m - 1, beat - 2)

                def x_b_between(beat, m=m):
                    if beat == (1 if m else 2):
                        if m:
                            pe.wait_ge(gate_open, 2 * m)
                        head_mean(N_QM + m, m + 1)
                    if m:
                        memory_head(m - 1, 4 + beat)

                unit(u, q_between, first=2 * KT if m == 0 else None)
                unit(u + 1, x_b_between)

            def head_unit(h, n, i=0):
                def between(beat):
                    b = 4 * n + beat
                    if h == 0:
                        if b == 0:
                            output(HM - 2, 1)
                        if b < 8:
                            memory_head(HM - 1, b)
                        if b == 8:
                            output(HM - 1, 1)
                        if b in (2, 3):
                            gate(HM - 1, b - 2)
                    if b in (5, 9):
                        if h == 0:
                            pe.wait_ge(gate_open, 2 * RT)
                        qk = b // 4 - 1
                        head_mean(N_HEAD + 2 * h + qk, HM + 2 * h + qk + 1, 4 * i)
                    if h >= 1:
                        band_head(h - 1, b, i)

                unit(U_HEAD + PER_H * h + n, between, 2 * PER_H * i)

            for h in range(2):
                for n in range(PER_H):
                    head_unit(h, n)
            with pe.Fori(0, 3) as i:
                for h in (2, 3):
                    for n in range(PER_H):
                        head_unit(h, n, i)
            for j in range(RT):
                unit(U_GB + j, lambda beat, j=j: band_head(HA - 1, 4 * j + beat),
                     stage_ends=j == RT - 1)
            for m in range(4):
                unit(U_OUT + m, first=3 * KT if m == 0 else None)
            with pe.Fori(0, 3) as i:
                for m in range(4):
                    unit(U_OUT + 4 + m, more=4 * i, stage_ends=m == 3)

            pe.wait_ge(flip_read, flips_before(HM + HA))

            def down(u, i=0):
                pe.wait_ge(lo_split, u + 1 + FF_PER * i)
                t0 = tiles_through(u) - DOWN_TILES
                w = [buf[:, u % 2, :].rearrange("p (k n) -> p k n", k=GROUP) for buf in (wh, wl)]
                for n in range(DOWN_TILES):
                    t = t0 + n
                    pe.wait_ge(tile_read, t - 3 + FF_TILES * i)
                    out = [slots[t % 4][:, c, 0:HALF] for c in range(2)]
                    for k in range(GROUP):
                        parts = [[x[:, k, c * HALF:(c + 1) * HALF] for c in range(2)] for x in (hh, hl)]
                        ins = products(out, [x[:, k, n * P:(n + 1) * P] for x in w], *parts,
                                       k == 0, k == GROUP - 1)
                    ins.then_inc(tile_ready, 1)

            def feed(g0, i=0):
                u = U_FF if g0 == 0 else U_LOOP
                for pos, (kind, j, _) in enumerate(ff_order(g0)):
                    if kind == "down":
                        if j == 0:
                            pe.wait_ge(h_lo, GROUP * g0 + GROUP * i)
                        down(u + pos, i)
                        continue
                    t = tiles_through(u + pos) - 1
                    if t == U_FF + 3:
                        pe.wait_ge(roots_ready, N_X1ROWS + 1)

                    def between(beat, t=t):
                        if t == U_FF and beat == 3:
                            pe.wait_ge(sums_ready, 3)
                            mean(N_X1ROWS, mean_rows[:], sum1)

                    unit(u + pos, between, FF_PER * i, first=4 * KT if t == U_FF else None,
                         tiles=FF_TILES * i, bank=t % 4)

            feed(0)
            with pe.Fori(0, NG - 1) as i:
                feed(1, i)

            pe.wait_ge(lo_split, U_LAST + 1)
            t0 = tiles_through(U_LAST - 1)
            w = [buf[:, U_LAST % 2, :].rearrange("p (k n) -> p k n", k=GROUP) for buf in (wh, wl)]
            for k in range(GROUP):
                pe.wait_ge(h_lo, GROUP * (NG - 1) + k + 1)
                parts = [[x[:, k, c * HALF:(c + 1) * HALF] for c in range(2)] for x in (hh, hl)]
                for n in range(DOWN_TILES):
                    if k == 0:
                        pe.wait_ge(tile_read, t0 + n - 3)
                    out = [slots[(t0 + n) % 4][:, c, 0:HALF] for c in range(2)]
                    ins = products(out, [x[:, k, n * P:(n + 1) * P] for x in w], *parts,
                                   k == 0, k == GROUP - 1)
                    if k == GROUP - 1:
                        ins.then_inc(tile_ready, 1)
            for q in range(1, DOWN):
                down(U_LAST + q)


_INS = ["xT", "memT", "cache_kT", "cache_v", "cache_mkT", "cache_mv", "params", "rel_table",
        "w_in", "w_mem_kv", "w_rg_a", "w_rg_i", "w_out", "w_up", "w_down"]
_OUTS = [("yT", (D, ROWS)), ("kT", (HA, P, ROWS)), ("vT", (HA, P, ROWS)), ("mkT", (HM, P, N_MEM)),
         ("mvT", (HM, P, N_MEM)), ("b_conv", (P, RT, 2 * (CB - 1))), ("b_h", (P, RT, 2)),
         ("f_conv", (P, 2 * FT, 4))]


def kernel(**inputs):
    import numpy as np
    import concourse.bacc as bacc
    from concourse import mybir as mb
    from concourse.bass_utils import run_bass_kernel_spmd

    a = {name: np.asarray(x) for name, x in inputs.items()}

    def tiles(x):
        x = x.reshape(*x.shape[:-1], x.shape[-1] // P, P)
        return np.moveaxis(x, -1, 0).reshape(P, -1)

    def past(x):
        x = x.reshape(x.shape[0], -1, P)
        return x.transpose(2, 1, 0).reshape(P, -1)

    parts = [tiles(a["g_attn"][0]), tiles(a["g_mem"][0]), tiles(a["g_ffn"][0]),
             tiles(a["g_q_a"][0]), tiles(a["g_k_a"][0]), tiles(a["g_q_m"][0]), tiles(a["g_k_m"][0]),
             tiles(a["conv_b_w"][0]), tiles(a["conv_b_b"][0]), tiles(a["b_rg_a"][0]),
             tiles(a["b_rg_i"][0]), tiles(a["lru_lambda"][0]), tiles(a["state_b_h"][0, 0]),
             past(a["cache_b_conv"][0, 0]), tiles(a["conv_f_w"][0]), tiles(a["conv_f_b"][0]),
             past(a["cache_f_conv"][0, 0])]
    laid = {
        "xT": np.concatenate([a["x_prompt"][0], a["x_sample"][0]]).T,
        "memT": a["mem_prompt"][0].T,
        "cache_kT": a["cache_a_k"][0, 0].transpose(1, 2, 0),
        "cache_v": a["cache_a_v"][0, 0],
        "cache_mkT": a["cache_mem_k"][0, 0].transpose(1, 2, 0),
        "cache_mv": a["cache_mem_v"][0, 0],
        "params": np.concatenate(parts, axis=1),
        "rel_table": a["rel_table"][0],
        **{name: a[name][0] for name in _INS[8:]},
    }
    nc = bacc.Bacc("TRN2", target_bir_lowering=False, num_devices=1)
    arrays, args = {}, []
    for name in _INS:
        x = np.ascontiguousarray(laid[name])
        arrays[f"in_{name}"] = x
        args.append(nc.dram_tensor(f"in_{name}", x.shape, mb.dt.from_np(x.dtype),
                                   kind="ExternalInput").ap())
    for name, shape in _OUTS:
        args.append(nc.dram_tensor(f"out_{name}", shape, mb.dt.from_np(np.dtype(np.float32)),
                                   kind="ExternalOutput").ap())
    encoder(nc, *args)
    r = run_bass_kernel_spmd(nc, [arrays], core_ids=[0]).results[0]
    y, k, v, mk, mv, bc, bh, fc = (r[f"out_{name}"] for name, _ in _OUTS)
    y = y.T
    k, v = k.transpose(2, 0, 1), v.transpose(2, 0, 1)
    mk, mv = mk.transpose(2, 0, 1), mv.transpose(2, 0, 1)

    def rows_of(x, n):
        return np.ascontiguousarray(x.transpose(2, 1, 0).reshape(n, -1))[None, None]

    return tuple(np.ascontiguousarray(x) for x in (
        y[None, :SEQ], y[None, SEQ:],
        k[None, None, :SEQ], v[None, None, :SEQ], mk[None, None], mv[None, None],
        rows_of(bc[:, :, :CB - 1], CB - 1), rows_of(bh[:, :, :1], 1)[:, :, 0],
        rows_of(fc[:, :, :CF - 1], CF - 1),
        k[None, None, SEQ:], v[None, None, SEQ:],
        rows_of(bc[:, :, CB - 1:], CB - 1), rows_of(bh[:, :, 1:], 1)[:, :, 0],
        rows_of(fc[:, :, CF - 1:], CF - 1)))
```
